# Optimizing a Trainium2 kernel written in Bass

```python
import math
import jax, jax.numpy as jnp
from jax import lax
import numpy as np

D_MODEL = 1024
BATCH = 1
SEQ = 512
DEPTH = 2

N_CONV_LAYERS = DEPTH // 2
N_ATTN_LAYERS = DEPTH - N_CONV_LAYERS

CONV_WIDTH = 31

WINDOW_DILATIONS = ((128, 1), (512, 4), (2048, 16))
N_GROUPS = len(WINDOW_DILATIONS)
HEADS_PER_GROUP = 8
HEAD_DIM = 128
GROUP_WIDTH = HEADS_PER_GROUP * HEAD_DIM
Q_WIDTH = N_GROUPS * GROUP_WIDTH
ATTN_OUT_WIDTH = HEADS_PER_GROUP * HEAD_DIM
ATTN_BLOCK = 128
ROPE_THETA = 500000.0
ROT_DIM = HEAD_DIM // 4
NEG_INF = -1e30

N_EXPERTS = 64
TOP_K = 8
EXPERT_DIM = 256
SHARED_DIM = 256
ROUTED_SCALE = 2.5
MOE_ROWS = 128

DEEPNORM_ALPHA = (2.0 * DEPTH) ** 0.25
DEEPNORM_BETA = (8.0 * DEPTH) ** -0.25
LN_EPS = 1e-5

kernel_name = "yoco_conformer_dilated_attn_moe"

def layernorm(x, g, b):
    x32 = x.astype(jnp.float32)
    mu = jnp.mean(x32, axis=-1, keepdims=True)
    var = jnp.mean(jnp.square(x32 - mu), axis=-1, keepdims=True)
    y = (x32 - mu) * lax.rsqrt(var + LN_EPS) * g.astype(jnp.float32) + b.astype(jnp.float32)
    return y.astype(x.dtype)

def rotary(t, positions):
    half = ROT_DIM // 2
    inv_freq = ROPE_THETA ** (-jnp.arange(half, dtype=jnp.float32) * 2.0 / ROT_DIM)
    ang = positions.astype(jnp.float32)[..., None] * inv_freq
    cos = jnp.cos(ang)[:, :, None, None, :]
    sin = jnp.sin(ang)[:, :, None, None, :]
    tr = t[..., :ROT_DIM].astype(jnp.float32)
    x1, x2 = tr[..., :half], tr[..., half:]
    rot = jnp.concatenate([x1 * cos - x2 * sin, x2 * cos + x1 * sin], axis=-1)
    return jnp.concatenate([rot.astype(t.dtype), t[..., ROT_DIM:]], axis=-1)

def conv_module(x, w_in, b_in, w_dw, b_dw, ln_g, ln_b, w_out, b_out):
    h = x @ w_in + b_in
    a, g = jnp.split(h, 2, axis=-1)
    h = a * jax.nn.sigmoid(g)
    h = lax.conv_general_dilated(
        h, w_dw[:, None, :].astype(h.dtype), window_strides=(1,),
        padding=[(CONV_WIDTH - 1, 0)], dimension_numbers=("NWC", "WIO", "NWC"),
        feature_group_count=D_MODEL) + b_dw
    h = jax.nn.silu(layernorm(h, ln_g, ln_b))
    return h @ w_out + b_out

def dilated_window_attention(q, k, v, dil, steps):
    B, S, H, Dh = q.shape
    L = S // dil
    nb = -(-L // ATTN_BLOCK)
    Lp = nb * ATTN_BLOCK

    def blocks(t):
        t = t.reshape(B, L, dil, H, Dh).transpose(0, 2, 1, 3, 4)
        t = jnp.pad(t, ((0, 0), (0, 0), (0, Lp - L), (0, 0), (0, 0)))
        return t.reshape(B, dil, nb, ATTN_BLOCK, H, Dh)

    def with_prev(t):
        prev = jnp.pad(t[:, :, :-1], ((0, 0), (0, 0), (1, 0), (0, 0), (0, 0), (0, 0)))
        return jnp.concatenate([prev, t], axis=3)

    qb = blocks(q)
    kc = with_prev(blocks(k))
    vc = with_prev(blocks(v))
    s = jnp.einsum("bgnqhd,bgnkhd->bgnhqk", qb, kc,
                   preferred_element_type=jnp.float32) * (1.0 / math.sqrt(Dh))
    qi = jnp.arange(ATTN_BLOCK)[:, None]
    kc_idx = jnp.arange(2 * ATTN_BLOCK)[None, :]
    dist = qi + ATTN_BLOCK - kc_idx
    band = (dist >= 0) & (dist <= steps)
    blk = jnp.arange(nb)[:, None, None]
    valid = band[None] & ((blk > 0) | (kc_idx[None] >= ATTN_BLOCK))
    s = jnp.where(valid[None, None, :, None], s, NEG_INF)
    m = jnp.max(s, axis=-1, keepdims=True)
    p = jnp.exp(s - m)
    l = jnp.sum(p, axis=-1)
    o = jnp.einsum("bgnhqk,bgnkhd->bgnhqd", p, vc.astype(jnp.float32)) / l[..., None]
    lse = m[..., 0] + jnp.log(l)
    o = o.transpose(0, 1, 2, 4, 3, 5).reshape(B, dil, Lp, H, Dh)[:, :, :L]
    o = o.transpose(0, 2, 1, 3, 4).reshape(B, S, H, Dh)
    lse = lse.transpose(0, 1, 2, 4, 3).reshape(B, dil, Lp, H)[:, :, :L]
    lse = lse.transpose(0, 2, 1, 3).reshape(B, S, H)
    return o, lse

def dilated_mixture_attention(x, positions, w_q, w_o, k, v):
    B, S, _ = x.shape
    q = rotary((x @ w_q).reshape(B, S, N_GROUPS, HEADS_PER_GROUP, HEAD_DIM), positions)
    outs, lses = [], []
    for g, (win, dil) in enumerate(WINDOW_DILATIONS):
        steps = win // dil
        assert steps <= ATTN_BLOCK
        o, lse = dilated_window_attention(q[:, :, g], k[:, :, g], v[:, :, g], dil, steps)
        outs.append(o)
        lses.append(lse)
    wts = jax.nn.softmax(jnp.stack(lses, axis=2), axis=2)
    o = jnp.einsum("bsgh,bsghd->bshd", wts, jnp.stack(outs, axis=2))
    return o.astype(x.dtype).reshape(B, S, ATTN_OUT_WIDTH) @ w_o

def moe_ffn(x, router_w, router_bias, w_gate, w_up, w_down, sw_gate, sw_up, sw_down):
    B, S, D = x.shape
    T = B * S
    xt = x.reshape(T, D)
    scores = jax.nn.sigmoid(jnp.dot(xt.astype(jnp.float32), router_w.astype(jnp.float32)))
    _, idx = lax.top_k(scores + router_bias.astype(jnp.float32), TOP_K)
    gate = jnp.take_along_axis(scores, idx, axis=-1)
    gate = gate / jnp.sum(gate, axis=-1, keepdims=True) * ROUTED_SCALE
    N = T * TOP_K
    e_flat = idx.reshape(N)
    tok_flat = jnp.arange(N, dtype=jnp.int32) // TOP_K
    g_flat = gate.reshape(N)
    order = jnp.argsort(e_flat)
    e_sorted = e_flat[order]
    counts = jnp.bincount(e_flat, length=N_EXPERTS)
    padded = (counts + MOE_ROWS - 1) // MOE_ROWS * MOE_ROWS
    starts = jnp.cumsum(counts) - counts
    pstarts = jnp.cumsum(padded) - padded
    dest = pstarts[e_sorted] + jnp.arange(N, dtype=jnp.int32) - starts[e_sorted]
    n_blocks = -(-N // MOE_ROWS) + N_EXPERTS
    P = n_blocks * MOE_ROWS
    row_tok = jnp.zeros((P,), jnp.int32).at[dest].set(tok_flat[order])
    row_gate = jnp.zeros((P,), jnp.float32).at[dest].set(g_flat[order])
    pends = jnp.cumsum(padded)
    blk_start = jnp.arange(n_blocks) * MOE_ROWS
    blk_exp = jnp.minimum(jnp.sum(pends[None, :] <= blk_start[:, None], axis=1), N_EXPERTS - 1)

    def expert_block(args):
        tok, e = args
        xb = xt[tok]
        h = jax.nn.silu(xb @ w_gate[e]) * (xb @ w_up[e])
        return h @ w_down[e]

    y = lax.map(expert_block, (row_tok.reshape(n_blocks, MOE_ROWS), blk_exp))
    y = y.reshape(P, D) * row_gate[:, None].astype(x.dtype)
    routed = jax.ops.segment_sum(y, row_tok, num_segments=T)
    shared = (jax.nn.silu(xt @ sw_gate) * (xt @ sw_up)) @ sw_down
    return (routed + shared).reshape(B, S, D)

def setup_inputs(seed: int = 0) -> dict:
    key = jax.random.key(seed)
    ks = iter(jax.random.split(key, 32))
    f32 = jnp.float32

    def nrm(shape, scale):
        return jax.random.normal(next(ks), shape, f32) * scale

    D = D_MODEL
    nA, nB = N_CONV_LAYERS, N_ATTN_LAYERS
    return {
        "x": nrm((BATCH, SEQ, D), 1.0),
        "positions": jnp.broadcast_to(jnp.arange(SEQ, dtype=jnp.int32), (BATCH, SEQ)),
        "ln1_g": 1.0 + nrm((DEPTH, D), 0.02),
        "ln1_b": nrm((DEPTH, D), 0.02),
        "ln2_g": 1.0 + nrm((DEPTH, D), 0.02),
        "ln2_b": nrm((DEPTH, D), 0.02),
        "conv_w_in": nrm((nA, D, 2 * D), D ** -0.5),
        "conv_b_in": nrm((nA, 2 * D), 0.02),
        "conv_w_dw": nrm((nA, CONV_WIDTH, D), CONV_WIDTH ** -0.5),
        "conv_b_dw": nrm((nA, D), 0.02),
        "conv_ln_g": 1.0 + nrm((nA, D), 0.02),
        "conv_ln_b": nrm((nA, D), 0.02),
        "conv_w_out": nrm((nA, D, D), D ** -0.5 * DEEPNORM_BETA),
        "conv_b_out": nrm((nA, D), 0.02),
        "w_kv": nrm((D, 2 * Q_WIDTH), D ** -0.5),
        "attn_w_q": nrm((nB, D, Q_WIDTH), D ** -0.5),
        "attn_w_o": nrm((nB, ATTN_OUT_WIDTH, D), ATTN_OUT_WIDTH ** -0.5 * DEEPNORM_BETA),
        "router_w": nrm((DEPTH, D, N_EXPERTS), D ** -0.5),
        "router_bias": nrm((DEPTH, N_EXPERTS), 0.01),
        "exp_w_gate": nrm((DEPTH, N_EXPERTS, D, EXPERT_DIM), D ** -0.5),
        "exp_w_up": nrm((DEPTH, N_EXPERTS, D, EXPERT_DIM), D ** -0.5),
        "exp_w_down": nrm((DEPTH, N_EXPERTS, EXPERT_DIM, D), EXPERT_DIM ** -0.5 * DEEPNORM_BETA),
        "sh_w_gate": nrm((DEPTH, D, SHARED_DIM), D ** -0.5),
        "sh_w_up": nrm((DEPTH, D, SHARED_DIM), D ** -0.5),
        "sh_w_down": nrm((DEPTH, SHARED_DIM, D), SHARED_DIM ** -0.5 * DEEPNORM_BETA),
    }

def reference(x, positions, ln1_g, ln1_b, ln2_g, ln2_b, conv_w_in, conv_b_in, conv_w_dw,
              conv_b_dw, conv_ln_g, conv_ln_b, conv_w_out, conv_b_out, w_kv, attn_w_q,
              attn_w_o, router_w, router_bias, exp_w_gate, exp_w_up, exp_w_down,
              sh_w_gate, sh_w_up, sh_w_down):
    B, S, _ = x.shape
    k_shared = None
    v_shared = None
    for layer in range(DEPTH):
        if layer < N_CONV_LAYERS:
            mix = conv_module(x, conv_w_in[layer], conv_b_in[layer], conv_w_dw[layer],
                              conv_b_dw[layer], conv_ln_g[layer], conv_ln_b[layer],
                              conv_w_out[layer], conv_b_out[layer])
        else:
            if layer == N_CONV_LAYERS:
                kv = (x @ w_kv).reshape(B, S, 2, N_GROUPS, HEADS_PER_GROUP, HEAD_DIM)
                k_shared = rotary(kv[:, :, 0], positions)
                v_shared = kv[:, :, 1]
            j = layer - N_CONV_LAYERS
            mix = dilated_mixture_attention(x, positions, attn_w_q[j], attn_w_o[j],
                                            k_shared, v_shared)
        x = layernorm(DEEPNORM_ALPHA * x + mix, ln1_g[layer], ln1_b[layer])
        ffn = moe_ffn(x, router_w[layer], router_bias[layer], exp_w_gate[layer],
                      exp_w_up[layer], exp_w_down[layer], sh_w_gate[layer],
                      sh_w_up[layer], sh_w_down[layer])
        x = layernorm(DEEPNORM_ALPHA * x + ffn, ln2_g[layer], ln2_b[layer])
    return x


_drawn_inputs = setup_inputs


def setup_inputs(seed=0):
    import zlib

    import numpy as np

    out = dict(_drawn_inputs(seed))
    spreads = {}
    factors = {'conv_ln_b': 2.699, 'conv_b_in': 2.946, 'conv_ln_g': 2.91}
    for name, (base, spread) in spreads.items():
        noise = np.random.default_rng([zlib.crc32(name.encode()), seed]).standard_normal(out[name].shape)
        drawn = base * np.exp(spread * noise) if base else spread * noise
        out[name] = __import__('jax').numpy.asarray(drawn.astype(out[name].dtype))
    for name, factor in factors.items():
        out[name] = (out[name] * factor).astype(out[name].dtype)
    return out
```

```python
from contextlib import ExitStack

import numpy as np

import concourse.bass as bass
from concourse import mybir

F32 = mybir.dt.float32
I32 = mybir.dt.int32
U32 = mybir.dt.uint32
F32R = mybir.dt.float32r
ALU = mybir.AluOpType
ACT = mybir.ActivationFunctionType
AXX = mybir.AxisListType.X

P = 128
D = 1024
KT = D // P
T = 512
NT = T // P
TAPS = 31
HEADS = 8
QW = 3 * D
E = 64
F = 256
TOPK = 8
OVER = 32
NB = E + OVER
CH = 2048
SLOTS = 6
ALPHA = float(4.0 ** 0.25)
EPS = 1e-5
NEG = -1e30
QSCALE = float(128 ** -0.5)
ROUTED_SCALE = 2.5
MAGIC = 12582912.0
TWO_PI = (6.28125, 0.0019350051879882812, 3.0198280420415554e-07)
PI_LO = 3.1415925


def build(nc, x, positions, ln1_g, ln1_b, ln2_g, ln2_b, conv_w_in, conv_b_in, conv_w_dw, conv_b_dw,
          conv_ln_g, conv_ln_b, conv_w_out, conv_b_out, w_kv, attn_w_q, attn_w_o, router_w, router_bias,
          exp_w_gate, exp_w_up, exp_w_down, sh_w_gate, sh_w_up, sh_w_down, inv_freq, out):
    xrows = nc.dram_tensor("xrows", [T, D], F32, kind="Internal").ap()
    acc = nc.dram_tensor("acc", [T + P, D], F32, kind="Internal").ap()
    etab = nc.dram_tensor("etab", [2, NB], I32, kind="Internal").ap()
    stat_ex = nc.dram_tensor("stat_ex", [2, T, 2 * HEADS], F32, kind="Internal").ap()

    ctx = ExitStack()
    with ctx:
        def sb(name, shape, dt=F32):
            return ctx.enter_context(nc.sbuf_tensor(name, shape, dt))

        def sem(name):
            return ctx.enter_context(nc.semaphore(name))

        W = sb("W", [P, SLOTS, CH])
        ident = sb("ident", [P, P])
        before = sb("before", [P, P])
        ones = sb("ones", [P, P])
        inv_d = sb("inv_d", [P, P])
        iota_f = sb("iota_f", [P, P])
        mask_near = sb("mask_near", [P, 256])
        mask_first = sb("mask_first", [P, 256])
        mask_far = sb("mask_far", [P, 256])
        imod = sb("imod", [P, P], I32)
        RW = sb("RW", [P, 2, KT, E])
        RB = sb("RB", [P, 2, E])
        LNG = sb("LNG", [P, D])
        LNB = sb("LNB", [P, D])
        cosT = sb("cosT", [32, T])
        sinT = sb("sinT", [32, T])
        vec_rows = sb("vec_rows", [40, P])
        vecT = sb("vecT", [P, 40])
        dwT = sb("dwT", [P, KT, TAPS])
        IDX = sb("IDX", [P, NB], U32)
        GTAB = sb("GTAB", [P, NB])
        IDXG = sb("IDXG", [P, 2], U32)
        IDXS = sb("IDXS", [P, 2], U32)
        base1 = sb("base1", [P, E])
        over_c = sb("over_c", [P, E])
        erow = sb("erow", [1, NB], I32)
        pcol = sb("pcol", [P, 8])
        sgn = sb("sgn", [32, 1])
        invf = sb("invf", [32, 1])
        eps = sb("eps", [P, 1])
        bns = sb("bns", [P, 2, 6])
        mv = sb("mv", [P, 2])
        rstd1 = sb("rstd1", [P, 1])
        std1 = sb("std1", [P, 1])
        small = sb("small", [P, 16])
        extra = sb("extra", [1, 1], I32)
        etmp = sb("etmp", [32, 2], I32)
        m8 = sb("m8", [P, NT, 8])
        s8 = sb("s8", [P, NT, 8])
        g8 = sb("g8", [P, NT, 8])
        s8i = sb("s8i", [P, NT * 8], I32)
        b8i = sb("b8i", [P, NT * 8], I32)
        p8i = sb("p8i", [P, NT * 8], I32)
        b8 = sb("b8", [P, NT * 8])
        p8 = sb("p8", [P, NT * 8])
        gsum = sb("gsum", [P, NT])
        grec = sb("grec", [P, NT])
        cnt = sb("cnt", [E, 4])
        cntB = sb("cntB", [E, P])
        obs = sb("obs", [P, E + 1])
        tabf = sb("tabf", [P, NB])
        delta = sb("delta", [P, E])
        statN = sb("statN", [P, 2, NT, 2 * HEADS])
        statP = sb("statP", [P, 2, NT, 2 * HEADS])
        wt = sb("wt", [P, 2, 4, NT, HEADS])
        mx = sb("mx", [P, NT])
        PS = ctx.enter_context(nc.psum_tensor("PS", [P, 8, 512], F32))

        with ExitStack() as layout:
            def sb1(name, shape, dt=F32):
                return layout.enter_context(nc.sbuf_tensor(name, shape, dt))

            X = sb1("X", [P, NT, D])
            XT = sb1("XT", [P, KT, T])
            BIG = sb1("BIG", [P, 23552])
        WL = [sb(f"WL{i}", [P, 2, CH], F32R) for i in range(2)]
        WH = sb("WH", [P, 2, 2, CH], F32R)
        XL = sb("XL", [P, 2, D], F32R)
        sb("between", [P, 15616 - 10240])
        XH = sb("XH", [P, 2, D], F32R)
        sb("behind", [P, 23552 - 17664])

        def big(at, *shape):
            n = int(np.prod(shape))
            ap = BIG[:, at:at + n]
            if len(shape) == 2:
                return ap.rearrange("p (a b) -> p a b", a=shape[0])
            if len(shape) == 3:
                return ap.rearrange("p (a b c) -> p a b c", a=shape[0], b=shape[1])
            return ap

        HALO = TAPS - 1
        HP = big(0, KT, HALO + T)
        Y = big(4352, KT, T)
        SG = big(8448, 2, T)
        SQ = big(9472, 2, T)
        RS = big(10496, T)
        DWR = BIG[0:TAPS, 11008:11008 + D]
        ROT = BIG[0:32, 16384:16384 + 4 * T].rearrange("p (a b) -> p a b", a=4)
        POSI = BIG[0:32, 18432:18432 + T]
        BOUT = big(15360, D)
        V = BIG[:, 0:12288].rearrange("p (g n c) -> p g n c", g=3, n=NT)
        O0 = big(12288, NT, D)
        XTP = big(12288, KT, T)
        O12 = big(0, NT, D)
        QT = big(16384, 2, 2, T)
        KTT = big(18432, 2, 2, T)
        PR = big(20480, NT, 256)
        PRT = big(21504, 8, P)
        RT = BIG[0:32, 22528:22528 + 2 * T].rearrange("p (a b) -> p a b", a=2)
        OT = big(4096, HEADS, T)
        SC, BI, BR, MK, GS, GT, SLM = (big(256 * i, NT, E) for i in range(7))
        EQ = BIG[:, 2048:4096].rearrange("p (n j e) -> p n j e", n=NT, j=8)
        EG = BIG[:, 4096:6144].rearrange("p (n j e) -> p n j e", n=NT, j=8)
        PJ = big(6144, 4, P)
        RR = big(6656, 4, 2 * NB)
        SLs = big(7424, 2, F)
        UPs = big(7936, 2, F)
        HSs = big(8448, 2, F)
        HTs = big(8960, 2, F)
        YS = big(9472, 2, D)
        AXB = big(11520, 2, D)
        XG = big(13568, 2, D)
        YB = big(17664, 2, D)
        SLm = big(19712, 2, F)
        Hm = big(20224, 2, F)
        HTm = big(20736, 2, F)

        s_vec, s_posd, s_zero, s_etab0 = sem("vec_loaded"), sem("pos_loaded"), sem("zeros_stored"), sem("etab_head")
        s_xin = [sem(f"x_loaded{n}") for n in range(NT)]
        s_rw = sem("router_loaded")
        s_gb = sem("ln_vectors_loaded")
        s_w = [sem(f"chunk{i}_loaded") for i in range(SLOTS)]
        s_cst = sem("constants_ready")
        s_pool = sem("pool_chain")
        s_dve = sem("dve_chain")
        s_act = sem("act_chain")
        s_vps, s_vev = sem("vectors_transposed"), sem("vectors_copied")
        s_ang, s_trig = sem("angles_ready"), sem("sines_ready")
        s_xps, s_xta, s_xtv = sem("x_transposed"), sem("xt_low_copied"), sem("xt_high_copied")
        s_ag, s_sg, s_h, s_y = sem("glu_products"), sem("glu_sigmoid"), sem("glu_out"), sem("conv_out")
        s_mu, s_yc, s_sq, s_vm = sem("mean_ready"), sem("centred"), sem("squared"), sem("variance_steps")
        s_std, s_t, s_z = sem("conv_std"), sem("conv_normed"), sem("conv_silu")
        s_mix = [sem(f"mix{i}_product") for i in range(2)]
        s_res = sem("residual_added")
        s_nvar, s_nstd, s_norm = sem("norm_variance"), sem("norm_std"), sem("norm_out")
        s_xr = [sem(f"xrows_stored{i}") for i in range(2)]
        s_rt = sem("router_logits")
        s_sc = sem("router_scores")
        s_mk = sem("router_mask")
        s_pos = [sem(f"ranks_ready{i}") for i in range(2)]
        s_cb = sem("counts_spread")
        s_ob = sem("overflow_bases")
        s_pj = [sem(f"onehots{i}") for i in range(2)]
        s_tb = [sem(f"table_steps{i}") for i in range(2)]
        s_tab = [sem(f"tables_ready{i}") for i in range(2)]
        s_et = [sem(f"etab_stored{i}") for i in range(2)]
        s_sgu = [sem(f"shared_gate_up{i}") for i in range(2)]
        s_ssl = [sem(f"shared_silu{i}") for i in range(2)]
        s_sh = [sem(f"shared_hidden{i}") for i in range(2)]
        s_sht = [sem(f"shared_hidden_T{i}") for i in range(2)]
        s_she = [sem(f"shared_hidden_T_copied{i}") for i in range(2)]
        s_sy = [sem(f"shared_product{i}") for i in range(2)]
        s_sye = [sem(f"shared_out{i}") for i in range(2)]
        s_ax = [sem(f"acc_tile{i}") for i in range(2)]
        s_acc = [[sem(f"acc_stored{i}_{k}") for k in range(2)] for i in range(2)]
        s_xg0 = [sem(f"gather_cleared{i}") for i in range(2)]
        s_mw = [[sem(f"expert_w{i}_{k}") for k in range(SLOTS)] for i in range(2)]
        s_ga = [[sem(f"gathered{i}_{k}") for k in range(2)] for i in range(2)]
        s_tx = [sem(f"gather_transposed{i}") for i in range(2)]
        s_xh = [sem(f"rows_high{i}") for i in range(2)]
        s_xl = [sem(f"rows_low{i}") for i in range(2)]
        s_wh = [sem(f"weights_high{i}") for i in range(2)]
        s_wl = [sem(f"weights_low{i}") for i in range(2)]
        s_gu = [sem(f"gate_up{i}") for i in range(2)]
        s_sl = [sem(f"expert_silu{i}") for i in range(2)]
        s_hd = [sem(f"expert_hidden{i}") for i in range(2)]
        s_ht = [sem(f"hidden_transposed{i}") for i in range(2)]
        s_he = [sem(f"hidden_T_copied{i}") for i in range(2)]
        s_yd = [sem(f"expert_out{i}") for i in range(2)]
        s_ya = [sem(f"expert_out_low_copied{i}") for i in range(2)]
        s_yv = [sem(f"expert_out_high_copied{i}") for i in range(2)]
        s_scat = [sem(f"scattered{i}") for i in range(2)]
        s_back = [sem(f"acc_loaded{i}") for i in range(2)]
        s_xtp = sem("xt_permuted")
        s_v, s_ve = sem("v_product"), sem("v_copied")
        s_qk, s_qke, s_rot, s_rots = sem("qk_product"), sem("qk_copied"), sem("qk_rotated"), sem("qk_shuffled")
        s_s, s_m, s_p = sem("scores_ready"), sem("row_max_ready"), sem("probs_ready")
        s_pt, s_pte = sem("probs_transposed"), sem("probs_T_copied")
        s_o, s_oe = sem("pv_product"), sem("pv_copied")
        s_st0, s_st1 = sem("stats_out"), sem("stats_in")
        s_ic = [sem(f"indices_copied{i}") for i in range(2)]
        s_go = [sem(f"indirect_dmas_released{i}") for i in range(2)]
        s_veh = sem("v_copied_odd")
        s_dve_w = sem("mix_exponents")
        s_wexp, s_wts = sem("mix_exp"), sem("mix_weighted")
        s_ot, s_ote = sem("heads_transposed"), sem("heads_T_copied")
        s_out = sem("out_stored")

        chunks = {}

        def wide(src, c):
            return src[:, c * F:(c + 1) * F].rearrange("(k p) n -> p k n", p=P)

        def down(src):
            return src.rearrange("(k p) n -> p k n", p=P)

        order = []
        for m in range(4):
            order += [(("a", m), wide(conv_w_in[0], m), 8, (s_ag, 2 * m + 2)),
                      (("g", m), wide(conv_w_in[0], 4 + m), 8, (s_ag, 2 * m + 2))]
        order += [(("co", m), wide(conv_w_out[0], m), 8, (s_mix[0], NT)) for m in range(4)]

        def shared(l):
            return [(("sg", l), wide(sh_w_gate[l], 0), 8, (s_sgu[l], NT)),
                    (("su", l), wide(sh_w_up[l], 0), 8, (s_sgu[l], NT)),
                    (("sd", l), down(sh_w_down[l]), 2, (s_sy[l], 2 * NT))]

        order += shared(0)
        n_first = len(order)
        for g in range(3):
            order += [(("v", g, m), wide(w_kv, (QW + g * D) // F + m), 8, (s_v, 8 * g + 4 * (m // 2) + 4))
                      for m in range(4)]
        for m in range(4):
            order += [(("q", 0, m), wide(attn_w_q[0], m), 8, (s_qk, 4 * m + 4)),
                      (("k", 0, m), wide(w_kv, m), 8, (s_qk, 4 * m + 4))]
        for m in range(4):
            for g in (1, 2):
                order += [(("q", g, m), wide(attn_w_q[0], 4 * g + m), 8, (s_qk, 2 * (8 + 4 * m + 2 + g))),
                          (("k", g, m), wide(w_kv, 4 * g + m), 8, (s_qk, 2 * (8 + 4 * m + 2 + g)))]
        order += [(("ao", m), wide(attn_w_o[0], m), 8, (s_mix[1], NT)) for m in range(4)]
        order += shared(1)
        count = [0] * SLOTS
        owner = [None] * SLOTS
        plan = []
        for i, (key, src, k, freed) in enumerate(order):
            slot = (i if i < n_first else i - n_first) % SLOTS
            count[slot] += 1
            plan.append((key, src, k, slot, None if i == n_first else owner[slot]))
            chunks[key] = (slot, 16 * count[slot])
            owner[slot] = freed
            if i == n_first - 1:
                freed_first = list(owner)
        freed_last = list(owner)

        def chunk(key, k=8):
            return W[:, chunks[key][0], :].rearrange("p (k n) -> p k n", k=k)

        def landed(eng, key):
            slot, value = chunks[key]
            eng.wait_ge(s_w[slot], value)

        def pair(key, k):
            s = chunks[key][0]
            return W[:, s:s + 2, k * F:(k + 1) * F]

        block = ctx.enter_context(nc.Block())

        @block.sync
        def _(sp):
            def load_chunk(i):
                key, src, k, slot, freed = plan[i]
                if freed is not None:
                    sp.wait_ge(*freed)
                sp.dma_start(W[:, slot, :].rearrange("p (k n) -> p k n", k=k), src).then_inc(s_w[slot], 16)

            def ln_vectors(r):
                if r:
                    sp.wait_ge(s_norm, NT * r)
                g, b = (ln1_g, ln1_b) if r % 2 == 0 else (ln2_g, ln2_b)
                sp.dma_start(LNG[:, :], g[r // 2:r // 2 + 1, :].broadcast_to([P, D])).then_inc(s_gb, 16)
                sp.dma_start(LNB[:, :], b[r // 2:r // 2 + 1, :].broadcast_to([P, D])).then_inc(s_gb, 16)

            def store_xrows(l):
                for n in range(NT):
                    sp.wait_ge(s_norm, 2 * NT * l + n + 1)
                    sp.dma_start(xrows[n * P:(n + 1) * P, :], X[:, n, :]).then_inc(s_xr[l], 16)

            def moe(l):
                freed = freed_first if l == 0 else freed_last

                def load(slot, e):
                    s, c = slot // 3, slot % 3
                    if c < 2:
                        src = (exp_w_gate, exp_w_up)[c][l, bass.ds(e, 1)].rearrange("e (k p) n -> p (e k) n", p=P)
                        dst = W[:, slot, :].rearrange("p (k n) -> p k n", k=KT)
                    else:
                        src = exp_w_down[l, bass.ds(e, 1)].rearrange("e (k p) n -> p (e k) n", p=P)
                        dst = W[:, slot, :].rearrange("p (k n) -> p k n", k=2)
                    sp.dma_start(dst, src).then_inc(s_mw[l][slot], 16)

                for slot in (3, 4, 5, 0, 1, 2):
                    sp.wait_ge(*freed[slot])
                    load(slot, slot // 3)
                for n in range(NT):
                    sp.wait_ge(s_ax[l], n + 1)
                    sp.dma_start(acc[n * P:(n + 1) * P, :], AXB[:, n % 2, :]).then_inc(s_acc[l][n % 2], 16)
                sp.wait_ge(s_tab[l], 2)
                sp.dma_start(etab[l, E:NB].rearrange("(a b) -> a b", b=1), etmp[:, 1:2]).then_inc(s_et[l], 16)
                sp.wait_ge(s_et[l], 16)
                n = sp.value_load(extra[0:1, 0:1], min_val=0, max_val=OVER // 2) + E // 2

                def load_gate_up(b, s):
                    e = sp.value_load(etab[l:l + 1, bass.ds(b, 1)], min_val=0, max_val=E - 1)
                    for c in range(2):
                        sp.wait_ge(s_wl[l], b * 2 - 3 + c)
                        load(3 * s + c, e)

                def load_down(b, s):
                    e = sp.value_load(etab[l:l + 1, bass.ds(b, 1)], min_val=0, max_val=E - 1)
                    sp.wait_ge(s_yd[l], b - 1)
                    load(3 * s + 2, e)

                load_gate_up(2, 0)
                with sp.Fori(0, n - 2) as it:
                    load_gate_up(it * 2 + 3, 1)
                    load_down(it * 2 + 2, 0)
                    load_gate_up(it * 2 + 4, 0)
                    load_down(it * 2 + 3, 1)
                load_gate_up(n * 2 - 1, 1)
                load_down(n * 2 - 2, 0)
                load_down(n * 2 - 1, 1)
                for t in range(NT):
                    if t == 0:
                        sp.wait_ge(s_scat[l], n * 32)
                    sp.dma_start(X[:, t, :], acc[t * P:(t + 1) * P, :]).then_inc(s_back[l], 16)
                return n

            for row, (v, k) in enumerate(((conv_b_in, 16), (conv_b_dw, 8), (conv_ln_g, 8), (conv_ln_b, 8))):
                at = (0, 16, 24, 32)[row]
                sp.dma_start(vec_rows[at:at + k, :], v.rearrange("a (k p) -> (a k) p", p=P)).then_inc(s_vec, 16)
            sp.dma_start(DWR, conv_w_dw[0]).then_inc(s_vec, 16)
            for n in range(NT):
                sp.dma_start(X[:, n, :], x[0, n * P:(n + 1) * P, :]).then_inc(s_xin[n], 16)
            load_chunk(0)
            load_chunk(1)
            sp.dma_start(POSI.bitcast(I32), positions.broadcast_to([32, T])).then_inc(s_posd, 16)
            sp.dma_start(invf[:, :], inv_freq).then_inc(s_posd, 16)
            for i in range(2, 6):
                load_chunk(i)
            sp.dma_start(BOUT, conv_b_out.broadcast_to([P, D])).then_inc(s_gb, 16)
            ln_vectors(0)
            for l in range(2):
                sp.dma_start(RW[:, l, :, :], router_w[l].rearrange("(k p) e -> p k e", p=P)).then_inc(s_rw, 16)
                sp.dma_start(RB[:, l, :], router_bias[l:l + 1, :].broadcast_to([P, E])).then_inc(s_rw, 16)
            sp.wait_ge(s_cst, 1)
            sp.dma_start(acc[T:T + P, :], XG[:, 0, :]).then_inc(s_zero, 16)
            for l in range(2):
                sp.dma_start(etab[l:l + 1, :], erow[:, :]).then_inc(s_etab0, 16)
            for i in range(6, n_first):
                load_chunk(i)
            store_xrows(0)
            ln_vectors(1)
            sp.wait_ge(s_etab0, 32)
            n0 = moe(0)
            sp.wait_ge(s_yd[0], n0 * 2)
            for i in range(n_first, n_first + SLOTS):
                load_chunk(i)
            ln_vectors(2)
            for i in range(n_first + SLOTS, len(plan)):
                if plan[i][0] == ("ao", 0):
                    sp.wait_ge(s_p, 4 * 16)
                    sp.wait_ge(s_m, 16)
                    sp.dma_start(stat_ex[0].rearrange("(n p) c -> p n c", p=P), statN[:, 0, :, :]).then_inc(s_st0, 16)
                    sp.dma_start(stat_ex[1].rearrange("(i j) c -> i j c", j=NT), statP[:, 1, :, :]).then_inc(s_st0, 16)
                    sp.wait_ge(s_st0, 32)
                    sp.dma_start(statP[:, 0, :, :], stat_ex[0].rearrange("(i j) c -> i j c", j=NT)).then_inc(s_st1, 16)
                    sp.dma_start(statN[:, 1, :, :], stat_ex[1].rearrange("(n p) c -> p n c", p=P)).then_inc(s_st1, 16)
                load_chunk(i)
            store_xrows(1)
            ln_vectors(3)
            moe(1)
            for n in range(NT):
                sp.wait_ge(s_norm, 3 * NT + n + 1)
                sp.dma_start(out[0, n * P:(n + 1) * P, :], X[:, n, :]).then_inc(s_out, 16)
            sp.wait_ge(s_out, 16 * NT)
            sp.wait_ge(s_zero, 16)

        @block.gpsimd
        def _(pool):
            chain = [0]

            def link(ins):
                chain[0] += 1
                ins.then_inc(s_pool, 1)
                pool.wait_ge(s_pool, chain[0])

            pool.memset(XG[:, 0, :], 0.0)
            pool.memset(ones[:, :], 1.0)
            pool.memset(inv_d[:, :], 1.0 / D)
            pool.memset(eps[:, :], EPS)
            pool.memset(HP[:, :, 0:HALO], 0.0)
            pool.iota(erow[:, :], [[1, NB]], base=0, channel_multiplier=0)
            pool.memset(ident[:, :], 0.0)
            pool.memset(mask_near[:, :], 0.0)
            pool.memset(mask_first[:, :], 0.0)
            pool.memset(sgn[:, :], 1.0)
            pool.iota(iota_f[:, :], [[1, P]], base=0, channel_multiplier=0, allow_small_or_imprecise_dtypes=True)
            pool.iota(pcol[:, 0:1], [[0, 1]], base=0, channel_multiplier=1, allow_small_or_imprecise_dtypes=True)
            pool.iota(pcol[:, 1:2], [[0, 1]], base=T + 1, channel_multiplier=1, allow_small_or_imprecise_dtypes=True)
            pool.iota(pcol[:, 2:2 + NT], [[P, NT]], base=1, channel_multiplier=1, allow_small_or_imprecise_dtypes=True)
            pool.iota(base1[:, :], [[P, E]], base=1, channel_multiplier=0, allow_small_or_imprecise_dtypes=True)
            pool.iota(over_c[:, :], [[-P, E]], base=P * (E - 1), channel_multiplier=0, allow_small_or_imprecise_dtypes=True)
            link(pool.iota(imod[:, :], [[-1, P]], base=P, channel_multiplier=1))
            pool.affine_select(out=ident[:, :], in_=ident[:, :], compare_op=ALU.not_equal, fill=1.0, base=0,
                               pattern=[[-1, P]], channel_multiplier=1)
            pool.affine_select(out=before[:, :], in_=ones[:, :], compare_op=ALU.is_gt, fill=0.0, base=0,
                               pattern=[[1, P]], channel_multiplier=-1)
            pool.affine_select(out=sgn[:, :], in_=sgn[:, :], compare_op=ALU.is_ge, fill=-1.0, base=-16,
                               pattern=[[0, 1]], channel_multiplier=1)
            pool.affine_select(out=mask_near[:, 0:P], in_=mask_near[:, 0:P], compare_op=ALU.is_ge, fill=NEG, base=0,
                               pattern=[[1, P]], channel_multiplier=-1)
            for m in (mask_near, mask_first):
                last = pool.affine_select(out=m[:, P:256], in_=m[:, P:256], compare_op=ALU.is_ge, fill=NEG, base=0,
                                          pattern=[[-1, P]], channel_multiplier=1)
            link(last)
            link(pool.memset(mask_first[:, 0:P], NEG))
            pool.memset(mask_far[:, 0:P], 0.0).then_inc(s_cst, 1)
            pool.wait_ge(s_cst, 1)
            pool.wait_ge(s_ang, 1)
            for h in range(2):
                pool.affine_select(out=mask_far[:, h * P:(h + 1) * P], in_=mask_far[:, h * P:(h + 1) * P],
                                   compare_op=ALU.is_ge, fill=NEG, base=0, pattern=[[-1, P]],
                                   channel_multiplier=1).then_inc(s_cst, 1)

            def moe(l):
                pool.wait_ge(s_norm, 2 * NT * l + NT)
                pool.wait_ge(s_zero, 16)
                link(pool.memset(XG[:, 0:2, :], 0.0))
                for n in range(NT):
                    pool.wait_ge(s_ssl[l], 2 * n + 2)
                    if n >= 2:
                        pool.wait_ge(s_sht[l], n - 1)
                    pool.tensor_tensor(HSs[:, n % 2, :], SLs[:, n % 2, :], UPs[:, n % 2, :], ALU.mult).then_inc(s_sh[l], 1)
                    if n >= 1:
                        mix_in(l, n - 1)
                mix_in(l, NT - 1)
                pool.wait_ge(s_tab[l], 2)
                pool.wait_ge(s_xr[l], 16 * NT)
                n = pool.value_load(extra[0:1, 0:1], min_val=0, max_val=OVER // 2) + E // 2

                def gather(b, s):
                    used64 = pool.value_load(IDX[64:65, bass.ds(b, 1)].bitcast(I32), min_val=0, max_val=T + P)
                    used96 = pool.value_load(IDX[96:97, bass.ds(b, 1)].bitcast(I32), min_val=0, max_val=T + P)
                    pool.tensor_copy(IDXG[:, s:s + 1], IDX[:, bass.ds(b, 1)]).then_inc(s_ic[l], 1)
                    pool.wait_ge(s_ic[l], b + 1 if isinstance(b, int) and b < 3 else b * 2 - 2)
                    pool.sem_inc(s_go[l], 1)

                    def rows(r):
                        pool.indirect_dma_start(XG[0:r, s, :], None, xrows,
                                                bass.IndirectOffsetOnAxis(IDXG[0:r, s:s + 1], axis=0),
                                                bounds_check=T - 1, oob_is_err=False).then_inc(s_ga[l][s], 16)

                    by_size(used64, used96, rows)

                def by_size(used64, used96, rows):
                    with pool.If(used64 < T):
                        with pool.If(used96 < T):
                            rows(P)
                        with pool.Else():
                            rows(96)
                        pool.sem_inc(s_go[l], 1)
                    with pool.Else():
                        rows(64)

                def scatter(b, s, copies):
                    used64 = pool.value_load(IDX[64:65, bass.ds(b, 1)].bitcast(I32), min_val=0, max_val=T + P)
                    used96 = pool.value_load(IDX[96:97, bass.ds(b, 1)].bitcast(I32), min_val=0, max_val=T + P)
                    pool.tensor_copy(IDXS[:, s:s + 1], IDX[:, bass.ds(b, 1)]).then_inc(s_ic[l], 1)
                    pool.wait_ge(s_ic[l], copies)
                    pool.wait_ge(s_ya[l], b + 1)
                    pool.wait_ge(s_yv[l], b + 1)
                    if not (isinstance(b, int) and b == 0):
                        pool.wait_ge(s_scat[l], b * 16)
                    pool.sem_inc(s_go[l], 1)

                    def rows(r):
                        pool.indirect_dma_start(acc, bass.IndirectOffsetOnAxis(IDXS[0:r, s:s + 1], axis=0), YB[0:r, s, :],
                                                None, compute_op=ALU.add).then_inc(s_scat[l], 16)

                    by_size(used64, used96, rows)

                gather(0, 0)
                gather(1, 1)
                pool.wait_ge(s_tx[l], 1)
                gather(2, 0)
                for k in range(2):
                    pool.wait_ge(s_acc[l][k], 16 * NT // 2)

                def step(b, s):
                    pool.wait_ge(s_tx[l], b + 2)
                    gather(b + 3, 1 - s)
                    scatter(b, s, b * 2 + 5)

                step(0, 0)
                step(1, 1)
                with pool.Fori(1, n - 2) as it:
                    step(it * 2, 0)
                    step(it * 2 + 1, 1)
                step(n * 2 - 4, 0)
                for k in range(3):
                    scatter(n * 2 - 3 + k, (1 + k) % 2, n * 4 - 2 + k)

            def mix_in(l, n):
                if n >= 2:
                    pool.wait_ge(s_acc[l][n % 2], 16 * (n // 2))
                link(pool.tensor_scalar(AXB[:, n % 2, :], X[:, n, :], ALPHA, None, ALU.mult))
                pool.wait_ge(s_sye[l], 2 * n + 2)
                pool.tensor_tensor(AXB[:, n % 2, :], AXB[:, n % 2, :], YS[:, n % 2, :], ALU.add).then_inc(s_ax[l], 1)

            moe(0)
            pool.wait_ge(s_xta, 3 * NT)
            pool.wait_ge(s_xtv, 3 * NT)
            for k in range(KT):
                pool.tensor_copy(XTP[:, k, :].rearrange("p (j i) -> p j i", j=NT),
                                 XT[:, k, :].rearrange("p (i j) -> p j i", j=NT)).then_inc(s_xtp, 1)
            moe(1)

        @block.scalar
        def _(act):
            A = nc.scalar.activation

            def xt_low(q):
                n = q % NT
                act.wait_ge(s_xps, q + 1)
                A(XT[:, 0:4, n * P:(n + 1) * P], PS[:, 4 + 2 * (n % 2), :].rearrange("p (k t) -> p k t", k=4),
                  ACT.Copy).then_inc(s_xta, 1)

            def norm_round(r):
                for n in range(NT):
                    act.wait_ge(s_nvar, NT * r + n + 1)
                    A(std1[:, :], mv[:, 1:2], ACT.Sqrt, bias=eps[:, :]).then_inc(s_nstd, 1)
                    if r < 3:
                        if n >= 1:
                            xt_low(NT * (r + 1) + n - 1)
                if r < 3:
                    xt_low(NT * (r + 1) + NT - 1)

            def moe(l):
                act.wait_ge(s_norm, 2 * NT * l + NT)
                act.wait_ge(s_rt, l + 1)
                A(SC, PS[:, 0, 0:256].rearrange("p (n e) -> p n e", n=NT), ACT.Sigmoid).then_inc(s_sc, 1)
                for n in range(NT + 1):
                    if n < NT:
                        act.wait_ge(s_sgu[l], n + 1)
                        if n >= 2:
                            act.wait_ge(s_sh[l], n - 1)
                        A(SLs[:, n % 2, :], PS[:, 4 + n % 2, 0:F], ACT.Silu).then_inc(s_ssl[l], 1)
                        A(UPs[:, n % 2, :], PS[:, 4 + n % 2, F:2 * F], ACT.Copy).then_inc(s_ssl[l], 1)
                    if n >= 1:
                        m = n - 1
                        act.wait_ge(s_sht[l], m + 1)
                        if m >= 2:
                            act.wait_ge(s_sy[l], 2 * (m - 1))
                        A(HTs[:, m % 2, :], PS[:, 6, 0:F], ACT.Copy).then_inc(s_she[l], 1)
                        for h in range(2):
                            act.wait_ge(s_sy[l], 2 * m + h + 1)
                            if m >= 2 and h == 0:
                                act.wait_ge(s_ax[l], m - 1)
                            A(YS[:, m % 2, h * 512:(h + 1) * 512], PS[:, 7 if h == 0 else 3, :], ACT.Copy).then_inc(s_sye[l], 1)
                act.wait_ge(s_tab[l], 2)
                n = act.value_load(extra[0:1, 0:1], min_val=0, max_val=OVER // 2) + E // 2

                act.wait_ge(s_ax[l], NT)
                act.wait_ge(s_xr[l], 16 * NT)

                def rows_high(b, s):
                    act.wait_ge(s_tx[l], b + 1)
                    A(XH[:, s, :], PS[:, 0:2, :].rearrange("p a t -> p (a t)"), ACT.Copy).then_inc(s_xh[l], 1)

                def weights_high(b, s, it):
                    for c in range(2):
                        act.wait_ge(s_mw[l][3 * s + c], it * 16 + 16)
                        A(WH[:, s, c, :], W[:, 3 * s + c, :], ACT.Copy).then_inc(s_wh[l], 1)

                def silu(b, s):
                    act.wait_ge(s_gu[l], b + 1)
                    A(SLm[:, s, :], PS[:, 3 + s, 0:F], ACT.Silu).then_inc(s_sl[l], 1)

                def out_low(b, s):
                    act.wait_ge(s_yd[l], b + 1)
                    if not (isinstance(b, int) and b < 2):
                        act.wait_ge(s_scat[l], (b - 1) * 16)
                    A(YB[:, s, 0:512], PS[:, 5, :], ACT.Copy).then_inc(s_ya[l], 1)

                def step(b, s, it, more):
                    if more:
                        weights_high(b + 2, s, it + 1)
                    if more or s == 0:
                        silu(b + 1, 1 - s)
                    if more:
                        rows_high(b + 2, s)
                    out_low(b, s)

                for s in range(2):
                    rows_high(s, s)
                    weights_high(s, s, 0)
                silu(0, 0)
                step(0, 0, 0, True)
                step(1, 1, 0, True)
                with act.Fori(1, n - 1) as it:
                    step(it * 2, 0, it, True)
                    step(it * 2 + 1, 1, it, True)
                step(n * 2 - 2, 0, None, False)
                step(n * 2 - 1, 1, None, False)

            act.wait_ge(s_vps, 1)
            A(vecT[:, :], PS[:, 0, 0:40], ACT.Copy).then_inc(s_vev, 1)
            A(dwT[:, :, :], PS[:, 1, 0:KT * TAPS].rearrange("p (k t) -> p k t", k=KT), ACT.Copy).then_inc(s_vev, 1)
            for n in range(NT):
                xt_low(n)
            act.wait_ge(s_vev, 2)
            for j in range(KT):
                act.wait_ge(s_ag, j + 1)
                if j >= 2:
                    act.wait_ge(s_h, j - 1)
                A(SG[:, j % 2, :], PS[:, 2 + j % 2, :], ACT.Sigmoid, bias=vecT[:, 8 + j:9 + j]).then_inc(s_sg, 1)
            act.wait_ge(s_ang, 3)
            A(sinT[:, :], ROT[:, 0, :], ACT.Sin).then_inc(s_trig, 1)
            A(cosT[:, :], ROT[:, 1, :], ACT.Sin).then_inc(s_trig, 1)
            for j in range(KT):
                act.wait_ge(s_yc, j + 1)
                if j >= 2:
                    act.wait_ge(s_vm, j - 1)
                A(SQ[:, j % 2, :], Y[:, j, :], ACT.Square).then_inc(s_sq, 1)
            act.wait_ge(s_vm, KT)
            A(RS, PS[:, 5, :], ACT.Sqrt, bias=eps[:, :]).then_inc(s_std, 1)
            for j in range(KT):
                act.wait_ge(s_t, j + 1)
                A(Y[:, j, :], Y[:, j, :], ACT.Silu, scale=vecT[:, 24 + j:25 + j], bias=vecT[:, 32 + j:33 + j]).then_inc(s_z, 1)
            norm_round(0)
            moe(0)
            norm_round(1)
            for c in range(3 * 2 * NT):
                if c % 2 == 0:
                    act.wait_ge(s_v, c + 1)
                    g, hf, n = c // 8, (c // 4) % 2, c % 4
                    A(V[:, g, n, hf * 512:(hf + 1) * 512], PS[:, c % 4, :], ACT.Copy).then_inc(s_ve, 1)

            def qk_copy(i, g, par, item):
                for w, dst in enumerate((QT, KTT)):
                    act.wait_ge(s_qk, 2 * i + w + 1)
                    o = dst[:, par, item, :]
                    if g == 0:
                        A(o, PS[:, w, :], ACT.Copy).then_inc(s_qke, 1)
                    else:
                        A(o.rearrange("p (j i) -> p j i", j=NT), PS[:, w, :].rearrange("p (i j) -> p j i", j=NT),
                          ACT.Copy).then_inc(s_qke, 1)

            def softmax(u):
                st = statN[:, 0] if u < 8 else statP[:, 1]
                h = u % 8
                act.wait_ge(s_m, u + 1)
                if u >= 1:
                    act.wait_ge(s_pt, u)
                for n in range(NT):
                    A(PR[:, n, :], PS[:, 2 + n // 2, (n % 2) * 256:(n % 2) * 256 + 256], ACT.Exp, scale=QSCALE,
                      bias=st[:, n, h:h + 1], accum_out=st[:, n, HEADS + h:HEADS + h + 1]).then_inc(s_p, 1)

            def probs_T(u):
                act.wait_ge(s_pt, u + 1)
                A(PRT[:, 0:4, :], PS[:, 4, :].rearrange("p (k t) -> p k t", k=4), ACT.Copy).then_inc(s_pte, 1)
                A(PRT[:, 4:8, :], PS[:, 5, :].rearrange("p (k t) -> p k t", k=4), ACT.Copy).then_inc(s_pte, 1)

            def items(u):
                return [(u, 0)] if u < 8 else [(8 + 2 * (u - 8), 1), (9 + 2 * (u - 8), 2)]

            for u in range(17):
                for k, (i, g) in enumerate(items(u) if u < 16 else []):
                    if u >= 2:
                        act.wait_ge(s_s, u - 1)
                    qk_copy(i, g, u % 2, k)
                if u >= 2:
                    probs_T(u - 2)
                if u >= 1:
                    softmax(u - 1)
            probs_T(15)
            act.wait_ge(s_st1, 32)
            for d in range(2):
                act.wait_ge(s_dve_w, 2 * d + 2)
                for k in range(2):
                    A(wt[:, d, k, :, :], wt[:, d, k, :, :], ACT.Exp).then_inc(s_wexp, 1)
            norm_round(2)
            moe(1)
            norm_round(3)

        @block.vector
        def _(dve):
            v = nc.vector
            chain = [0]

            def link(ins):
                chain[0] += 1
                ins.then_inc(s_dve, 1)
                dve.wait_ge(s_dve, chain[0])

            def xt_high(q):
                n = q % NT
                dve.wait_ge(s_xps, q + 1)
                v.tensor_copy(XT[:, 4:8, n * P:(n + 1) * P],
                              PS[:, 5 + 2 * (n % 2), :].rearrange("p (k t) -> p k t", k=4)).then_inc(s_xtv, 1)

            def norm_round(r):
                dve.wait_ge(s_gb, 16 + 32 * (r + 1))
                for n in range(NT):
                    if r % 2 == 0:
                        l = r // 2
                        dve.wait_ge(s_mix[l], n + 1)
                        b = 2 * (n % 2)
                        link(v.scalar_tensor_tensor(X[:, n, :].rearrange("p (a b) -> p a b", a=2),
                                                    X[:, n, :].rearrange("p (a b) -> p a b", a=2), ALPHA,
                                                    PS[:, b:b + 2, :], ALU.mult, ALU.add))
                        if l == 0:
                            link(v.tensor_tensor(X[:, n, :], X[:, n, :], BOUT, ALU.add))
                    elif n == 0:
                        dve.wait_ge(s_back[r // 2], 16 * NT)
                    for h in range(2):
                        last = v.bn_stats(bns[:, h, :], X[:, n, h * 512:(h + 1) * 512])
                    link(last)
                    v.bn_aggr(mv[:, :], bns[:, :, :]).then_inc(s_nvar, 1)
                    dve.wait_ge(s_nstd, NT * r + n + 1)
                    link(v.reciprocal(rstd1[:, :], std1[:, :]))
                    link(v.tensor_scalar(X[:, n, :], X[:, n, :], mv[:, 0:1], rstd1[:, :], ALU.subtract, ALU.mult))
                    link(v.tensor_tensor(X[:, n, :], X[:, n, :], LNG[:, :], ALU.mult))
                    v.tensor_tensor(X[:, n, :], X[:, n, :], LNB[:, :], ALU.add).then_inc(s_norm, 1)
                    if r < 3 and n >= 1:
                        xt_high(NT * (r + 1) + n - 1)
                if r < 3:
                    xt_high(NT * (r + 1) + NT - 1)

            def route(l):
                dve.wait_ge(s_norm, 2 * NT * l + NT)
                dve.wait_ge(s_rw, 64)
                dve.wait_ge(s_sc, l + 1)
                rb = RB[:, l:l + 1, :].broadcast_to([P, NT, E])
                link(v.tensor_tensor(BI, SC, rb, ALU.add))
                for n in range(NT):
                    last = v.max(m8[:, n, :], BI[:, n, :])
                link(last)
                for n in range(NT):
                    last = v.match_replace(BR[:, n, :], m8[:, n, :], BI[:, n, :], NEG)
                link(last)
                v.tensor_tensor(MK, BI, BR, ALU.not_equal).then_inc(s_mk, 1)
                dve.wait_ge(s_mk, l + 1)
                link(v.tensor_tensor(GS, SC, MK, ALU.mult))
                link(v.tensor_reduce(gsum[:, :], GS, AXX, ALU.add))
                link(v.reciprocal(grec[:, :], gsum[:, :]))
                link(v.tensor_scalar(grec[:, :], grec[:, :], ROUTED_SCALE, None, ALU.mult))
                link(v.tensor_tensor(GT, GS, grec[:, :].unsqueeze(2).broadcast_to([P, NT, E]), ALU.mult))
                dve.wait_ge(s_pos[l], 2)
                for k in range(3):
                    last = v.tensor_scalar(cnt[:, k:k + 1], PS[0:E, 2, 0:1], float(P * (k + 1)), None, ALU.is_gt)
                link(last)
                link(v.tensor_tensor(cnt[:, 3:4], cnt[:, 0:1], cnt[:, 1:2], ALU.add))
                link(v.tensor_tensor(cnt[:, 3:4], cnt[:, 3:4], cnt[:, 2:3], ALU.add))
                v.tensor_scalar(cntB[:, :], ones[0:E, :], cnt[:, 3:4], None, ALU.mult).then_inc(s_cb, 1)
                dve.wait_ge(s_ob, l + 1)
                link(v.tensor_copy(obs[:, :], PS[:, 2, 128:129 + E]))
                link(v.scalar_tensor_tensor(delta[:, :], obs[:, 0:E], float(P), over_c[:, :], ALU.mult, ALU.add))
                pos = PS[:, 1, 0:256].rearrange("p (n e) -> p n e", n=NT)
                link(v.scalar_tensor_tensor(SLM, pos, float(P), delta[:, :].unsqueeze(1).broadcast_to([P, NT, E]),
                                            ALU.is_ge, ALU.mult))
                link(v.tensor_tensor(SLM, SLM, pos, ALU.add))
                link(v.tensor_tensor(SLM, SLM, base1[:, :].unsqueeze(1).broadcast_to([P, NT, E]), ALU.add))
                link(v.tensor_tensor(SLM, SLM, MK, ALU.mult))
                for n in range(NT):
                    last = v.max(s8[:, n, :], SLM[:, n, :])
                link(last)
                for n in range(NT):
                    last = v.tensor_tensor(EQ[:, n], SLM[:, n:n + 1, :].broadcast_to([P, 8, E]),
                                           s8[:, n, :].unsqueeze(2).broadcast_to([P, 8, E]), ALU.is_equal)
                link(last)
                for n in range(NT):
                    last = v.tensor_tensor(EG[:, n], EQ[:, n], GT[:, n:n + 1, :].broadcast_to([P, 8, E]), ALU.mult)
                link(last)
                link(v.tensor_reduce(g8[:, :, :], EG, AXX, ALU.add))
                s8f = s8[:, :, :].rearrange("p n j -> p (n j)")
                link(v.tensor_scalar(s8i[:, :], s8f, -1.0, None, ALU.add))
                v.tensor_scalar(b8i[:, :], s8i[:, :], 7, None, ALU.logical_shift_right)
                link(v.tensor_scalar(p8i[:, :], s8i[:, :], 127, None, ALU.bitwise_and))
                v.tensor_copy(b8[:, :], b8i[:, :])
                link(v.tensor_copy(p8[:, :], p8i[:, :]))
                for i in range(NT * 8):
                    if i >= 4:
                        dve.wait_ge(s_tb[l], i - 3)
                    v.tensor_scalar(PJ[:, i % 4, :], iota_f[:, :], p8[:, i:i + 1], None, ALU.is_equal)
                    v.tensor_scalar(RR[:, i % 4, 0:NB], iota_f[:, 0:NB], b8[:, i:i + 1], pcol[:, 2 + i // 8:3 + i // 8],
                                    ALU.is_equal, ALU.mult)
                    v.tensor_scalar(RR[:, i % 4, NB:2 * NB], iota_f[:, 0:NB], b8[:, i:i + 1],
                                    g8[:, i // 8, i % 8:i % 8 + 1], ALU.is_equal, ALU.mult).then_inc(s_pj[l], 1)
                v.tensor_scalar(tabf[0:32, 0:E], obs[0:32, 1:E + 1], pcol[0:32, 0:1], 0.0,
                                ALU.is_le, ALU.add, accum_out=small[0:32, 0:1])
                link(v.tensor_scalar(small[0:1, 1:2], obs[0:1, E:E + 1], 1.0, None, ALU.add))
                link(v.tensor_scalar(small[0:1, 2:3], small[0:1, 1:2], 0.0, None, ALU.add))
                link(v.tensor_scalar(etmp[:, 1:2], small[0:32, 0:1], float(E - 1), None, ALU.min))
                link(v.tensor_scalar(etmp[0:1, 0:1], small[0:1, 2:3], 0.0, None, ALU.add))
                v.tensor_scalar(extra[0:1, 0:1], etmp[0:1, 0:1], 1, None, ALU.logical_shift_right).then_inc(s_tab[l], 1)
                dve.wait_ge(s_tb[l], NT * 8)
                link(v.tensor_scalar(tabf[:, :], PS[:, 0, 256:256 + NB], 0.0, pcol[:, 1:2],
                                     ALU.is_equal, ALU.mult))
                link(v.tensor_tensor(tabf[:, :], tabf[:, :], PS[:, 0, 256:256 + NB], ALU.add))
                link(v.tensor_copy(GTAB[:, :], PS[:, 0, 256 + NB:256 + 2 * NB]))
                v.tensor_scalar(IDX[:, :], tabf[:, :], -1.0, None, ALU.add).then_inc(s_tab[l], 1)

            def moe(l):
                route(l)
                dve.wait_ge(s_tab[l], 2)
                n = dve.value_load(extra[0:1, 0:1], min_val=0, max_val=OVER // 2) + E // 2

                dve.wait_ge(s_ax[l], NT)
                dve.wait_ge(s_xr[l], 16 * NT)

                def rows_low(b, s):
                    dve.wait_ge(s_xh[l], b + 1)
                    v.tensor_tensor(XL[:, s, :], PS[:, 0:2, :].rearrange("p a t -> p (a t)"), XH[:, s, :].bitcast(F32),
                                    ALU.subtract).then_inc(s_xl[l], 1)

                def weights_low(b, s):
                    for c in range(2):
                        dve.wait_ge(s_wh[l], b * 2 + 1 + c)
                        v.tensor_tensor(WL[s][:, c, :], W[:, 3 * s + c, :], WH[:, s, c, :].bitcast(F32),
                                        ALU.subtract).then_inc(s_wl[l], 1)

                def hidden(b, s):
                    dve.wait_ge(s_sl[l], b + 1)
                    if not (isinstance(b, int) and b < 2):
                        dve.wait_ge(s_ht[l], b - 1)
                    v.scalar_tensor_tensor(Hm[:, s, :], SLm[:, s, :], GTAB[:, bass.ds(b, 1)], PS[:, 3 + s, F:2 * F],
                                           ALU.mult, ALU.mult).then_inc(s_hd[l], 1)

                def hidden_T(b, s):
                    dve.wait_ge(s_ht[l], b + 1)
                    v.tensor_copy(HTm[:, s, :], PS[:, 2, 0:F]).then_inc(s_he[l], 1)

                def out_high(b, s):
                    dve.wait_ge(s_yd[l], b + 1)
                    if not (isinstance(b, int) and b < 2):
                        dve.wait_ge(s_scat[l], (b - 1) * 16)
                    v.tensor_copy(YB[:, s, 512:D], PS[:, 6, :]).then_inc(s_yv[l], 1)

                def step(b, s, more):
                    hidden_T(b, s)
                    if more:
                        weights_low(b + 2, s)
                    if more or s == 0:
                        hidden(b + 1, 1 - s)
                    if more:
                        rows_low(b + 2, s)
                    out_high(b, s)

                for s in range(2):
                    rows_low(s, s)
                    weights_low(s, s)
                hidden(0, 0)
                step(0, 0, True)
                step(1, 1, True)
                with dve.Fori(1, n - 1) as it:
                    step(it * 2, 0, True)
                    step(it * 2 + 1, 1, True)
                step(n * 2 - 2, 0, False)
                step(n * 2 - 1, 1, False)

            for n in range(NT):
                xt_high(n)
            dve.wait_ge(s_pool, 1)
            link(v.tensor_scalar(imod[:, :], imod[:, :], 3, None, ALU.bitwise_and))
            v.tensor_scalar(mask_far[:, P:256], imod[:, :], 0.0, NEG, ALU.not_equal, ALU.mult).then_inc(s_ang, 1)
            dve.wait_ge(s_posd, 32)
            link(v.tensor_copy(ROT[:, 2, :], POSI.bitcast(I32)))
            link(v.tensor_scalar(ROT[:, 2, :], ROT[:, 2, :], invf[:, :], None, ALU.mult))
            link(v.tensor_scalar(ROT[:, 3, :], ROT[:, 2, :], float(1.0 / (2.0 * np.pi)), None, ALU.mult))
            link(v.tensor_scalar(ROT[:, 3, :], ROT[:, 3, :], MAGIC, None, ALU.add))
            link(v.tensor_scalar(ROT[:, 3, :], ROT[:, 3, :], MAGIC, None, ALU.subtract))
            for c in TWO_PI:
                link(v.scalar_tensor_tensor(ROT[:, 2, :], ROT[:, 3, :], -c, ROT[:, 2, :], ALU.mult, ALU.add))
            v.tensor_scalar(ROT[:, 0, :], ROT[:, 2, :], -PI_LO, PI_LO, ALU.max, ALU.min).then_inc(s_ang, 1)
            link(v.tensor_scalar(ROT[:, 1, :], ROT[:, 2, :], float(np.pi / 2), None, ALU.add))
            link(v.tensor_scalar(ROT[:, 3, :], ROT[:, 1, :], float(np.pi), float(-2.0 * np.pi), ALU.is_gt, ALU.mult))
            link(v.tensor_tensor(ROT[:, 1, :], ROT[:, 1, :], ROT[:, 3, :], ALU.add))
            v.tensor_scalar(ROT[:, 1, :], ROT[:, 1, :], -PI_LO, PI_LO, ALU.max, ALU.min).then_inc(s_ang, 1)
            dve.wait_ge(s_cst, 1)
            dve.wait_ge(s_vev, 2)
            for j in range(KT):
                dve.wait_ge(s_sg, j + 1)
                v.scalar_tensor_tensor(HP[:, j, HALO:], PS[:, j % 2, :], vecT[:, j:j + 1], SG[:, j % 2, :],
                                       ALU.add, ALU.mult).then_inc(s_h, 1)
                dve.wait_ge(s_h, j + 1)
                link(v.tensor_scalar(Y[:, j, :], HP[:, j, 0:T], dwT[:, j, 0:1], vecT[:, 16 + j:17 + j], ALU.mult, ALU.add))
                for w in range(1, TAPS):
                    ins = v.scalar_tensor_tensor(Y[:, j, :], HP[:, j, w:w + T], dwT[:, j, w:w + 1], Y[:, j, :],
                                                 ALU.mult, ALU.add)
                    if w < TAPS - 1:
                        link(ins)
                    else:
                        ins.then_inc(s_y, 1)
            dve.wait_ge(s_mu, 1)
            for j in range(KT):
                v.tensor_tensor(Y[:, j, :], Y[:, j, :], PS[:, 4, :], ALU.subtract).then_inc(s_yc, 1)
            dve.wait_ge(s_std, 1)
            link(v.reciprocal(RS, RS))
            for j in range(KT):
                dve.wait_ge(s_sq, KT)
                v.tensor_tensor(Y[:, j, :], Y[:, j, :], RS, ALU.mult).then_inc(s_t, 1)
            norm_round(0)
            moe(0)
            norm_round(1)
            dve.wait_ge(s_trig, 2)
            link(v.tensor_scalar(sinT[:, :], sinT[:, :], sgn[:, :], None, ALU.mult))
            for c in range(3 * 2 * NT):
                if c % 2 == 1:
                    dve.wait_ge(s_v, c + 1)
                    g, hf, n = c // 8, (c // 4) % 2, c % 4
                    v.tensor_copy(V[:, g, n, hf * 512:(hf + 1) * 512], PS[:, c % 4, :]).then_inc(s_veh, 1)

            def rotate(i, g, par, item):
                swap = list(range(16, 32)) + list(range(16))
                for w, dst in enumerate((QT, KTT)):
                    dve.wait_ge(s_qke, 2 * i + w + 1)
                    src = dst[0:32, par, item, :]
                    cs, sn = cosT[:, :], sinT[:, :]
                    r0, r1 = RT[:, 0, :], RT[:, 1, :]
                    if g:
                        cs = cs.rearrange("p (i j) -> p j i", j=NT)
                        sn = sn.rearrange("p (i j) -> p j i", j=NT)
                        r0 = r0.rearrange("p (j i) -> p j i", j=NT)
                        r1 = r1.rearrange("p (j i) -> p j i", j=NT)
                        srcv = src.rearrange("p (j i) -> p j i", j=NT)
                    else:
                        srcv = src
                    if 2 * i + w:
                        dve.wait_ge(s_rot, 2 * i + w)
                    v.stream_shuffle(RT[:, 0, :], src, swap)
                    link(v.tensor_tensor(r1, srcv, cs, ALU.mult))
                    link(v.tensor_tensor(r0, r0, sn, ALU.mult))
                    v.tensor_tensor(src, RT[:, 0, :], RT[:, 1, :], ALU.add).then_inc(s_rot, 1)

            def row_max(u):
                st = statN[:, 0] if u < 8 else statP[:, 1]
                h = u % 8
                S = PS[:, 2:4, :].rearrange("p a (n c) -> p (a n) c", n=2)
                dve.wait_ge(s_s, u + 1)
                if u < 8:
                    v.tensor_tensor(S[:, 0, :], S[:, 0, :], mask_first[:, :], ALU.add)
                    link(v.tensor_tensor(S[:, 1:4, :], S[:, 1:4, :], mask_near[:, :].unsqueeze(1).broadcast_to([P, 3, 256]),
                                         ALU.add))
                else:
                    link(v.tensor_tensor(S, S, mask_far[:, :].unsqueeze(1).broadcast_to([P, 4, 256]), ALU.add))
                link(v.tensor_reduce(mx[:, :], S, AXX, ALU.max))
                v.tensor_scalar(st[:, :, h], mx[:, :], -QSCALE, None, ALU.mult).then_inc(s_m, 1)

            def pv_copy(u):
                dst = O0 if u < 8 else O12
                h = u % 8
                dve.wait_ge(s_o, u + 1)
                v.tensor_copy(dst[:, :, h * P:(h + 1) * P], PS[:, 6, :].rearrange("p (n d) -> p n d", n=NT)).then_inc(s_oe, 1)

            def items(u):
                return [(u, 0)] if u < 8 else [(8 + 2 * (u - 8), 1), (9 + 2 * (u - 8), 2)]

            for u in range(17):
                for k, (i, g) in enumerate(items(u) if u < 16 else []):
                    rotate(i, g, u % 2, k)
                if u >= 1:
                    row_max(u - 1)
                if u >= 2:
                    pv_copy(u - 2)
            pv_copy(15)
            dve.wait_ge(s_st1, 32)
            dve.wait_ge(s_p, 64)
            for d, st in enumerate((statN, statP)):
                link(v.tensor_tensor(wt[:, d, 2], st[:, 0, :, 0:HEADS], st[:, 1, :, 0:HEADS], ALU.min))
                for k in range(2):
                    v.tensor_tensor(wt[:, d, k], wt[:, d, 2], st[:, k, :, 0:HEADS], ALU.subtract).then_inc(s_dve_w, 1)
            for d, st in enumerate((statN, statP)):
                dve.wait_ge(s_wexp, 2 * d + 2)
                for k in range(2):
                    last = v.tensor_tensor(wt[:, d, 2 + k], wt[:, d, k], st[:, k, :, HEADS:2 * HEADS], ALU.mult)
                link(last)
                link(v.tensor_tensor(wt[:, d, 2], wt[:, d, 2], wt[:, d, 3], ALU.add))
                link(v.reciprocal(wt[:, d, 2], wt[:, d, 2]))
                link(v.tensor_tensor(wt[:, d, 3], wt[:, d, d], wt[:, d, 2], ALU.mult))
            for d, o in enumerate((O0, O12)):
                for n in range(NT):
                    on = o[:, n, :].rearrange("p (h c) -> p h c", h=HEADS)
                    v.tensor_tensor(on, on, wt[:, d, 3, n, :].unsqueeze(2).broadcast_to([P, HEADS, P]),
                                    ALU.mult).then_inc(s_wts, 1)
            for c in range(2 * NT):
                d, n = c // NT, c % NT
                for hf in range(2):
                    dve.wait_ge(s_ot, 2 * c + hf + 1)
                    src = PS[:, 4 + 2 * (c % 2) + hf, :].rearrange("p (h t) -> p h t", h=4)
                    if d == 0:
                        v.tensor_copy(OT[:, 4 * hf:4 * hf + 4, n * P:(n + 1) * P], src).then_inc(s_ote, 1)
                    else:
                        if n == 0 and hf == 0:
                            dve.wait_ge(s_ote, 2 * NT)
                        dst = OT[:, 4 * hf:4 * hf + 4, :].rearrange("p h (i j) -> p h j i", j=NT)[:, :, n, :]
                        v.tensor_tensor(dst, dst, src, ALU.add).then_inc(s_ote, 1)
            norm_round(2)
            moe(1)
            norm_round(3)

        @block.tensor
        def _(pe):
            mm = nc.tensor.matmul

            def x_T(q):
                r, n = q // NT, q % NT
                if r == 0:
                    pe.wait_ge(s_xin[n], 16)
                else:
                    pe.wait_ge(s_norm, NT * (r - 1) + n + 1)
                if q >= 2:
                    pe.wait_ge(s_xta, q - 1)
                    pe.wait_ge(s_xtv, q - 1)
                for k in range(KT):
                    last = nc.tensor.transpose(PS[:, 4 + 2 * (n % 2) + k // 4, (k % 4) * P:(k % 4 + 1) * P],
                                               X[:, n, k * P:(k + 1) * P], ident[:, :])
                last.then_inc(s_xps, 1)

            def out_proj(l, lhs, key):
                for c in range(4):
                    landed(pe, (key, c))
                for n in range(NT):
                    if n >= 2:
                        pe.wait_ge(s_norm, 2 * NT * l + n - 1)
                    for h in range(2):
                        for k in range(KT):
                            last = mm(PS[:, 2 * (n % 2) + h, :].rearrange("p (a b) -> p a b", a=2),
                                      lhs[:, k, n * P:(n + 1) * P], pair((key, 2 * h), k), start=(k == 0), stop=(k == KT - 1))
                    last.then_inc(s_mix[l], 1)

            def moe(l):
                pe.wait_ge(s_xta, NT * (2 * l + 2))
                pe.wait_ge(s_xtv, NT * (2 * l + 2))
                pe.wait_ge(s_rw, 64)
                for n in range(NT):
                    for k in range(KT):
                        last = mm(PS[:, 0, n * E:(n + 1) * E], XT[:, k, n * P:(n + 1) * P], RW[:, l, k, :],
                                  start=(k == 0), stop=(k == KT - 1))
                last.then_inc(s_rt, 1)

                def sh_gate_up(n):
                    if n == 0:
                        landed(pe, ("sg", l))
                        landed(pe, ("su", l))
                    if n >= 2:
                        pe.wait_ge(s_ssl[l], 2 * (n - 1))
                    for k in range(KT):
                        last = mm(PS[:, 4 + n % 2, :].rearrange("p (a b) -> p a b", a=2), XT[:, k, n * P:(n + 1) * P],
                                  pair(("sg", l), k), start=(k == 0), stop=(k == KT - 1))
                    last.then_inc(s_sgu[l], 1)

                def sh_down(n):
                    if n == 0:
                        landed(pe, ("sd", l))
                    pe.wait_ge(s_sh[l], n + 1)
                    if n >= 1:
                        pe.wait_ge(s_she[l], n)
                    for k in range(2):
                        last = nc.tensor.transpose(PS[:, 6, k * P:(k + 1) * P], HSs[:, n % 2, k * P:(k + 1) * P], ident[:, :])
                    last.then_inc(s_sht[l], 1)
                    pe.wait_ge(s_she[l], n + 1)
                    wd = chunk(("sd", l), 2)
                    for h in range(2):
                        if n >= 1:
                            pe.wait_ge(s_sye[l], 2 * (n - 1) + h + 1)
                        for k in range(2):
                            last = mm(PS[:, 7 if h == 0 else 3, :], HTs[:, n % 2, k * P:(k + 1) * P],
                                      wd[:, k, h * 512:(h + 1) * 512], start=(k == 0), stop=(k == 1))
                        last.then_inc(s_sy[l], 1)

                sh_gate_up(0)
                sh_gate_up(1)
                pe.wait_ge(s_mk, l + 1)
                for n in range(NT):
                    for m in range(n):
                        mm(PS[:, 1, n * E:(n + 1) * E], ones[:, :], MK[:, m, :], start=(m == 0), stop=False)
                    last = mm(PS[:, 1, n * E:(n + 1) * E], before[:, :], MK[:, n, :], start=(n == 0), stop=True)
                last.then_inc(s_pos[l], 1)
                for n in range(NT):
                    last = mm(PS[0:E, 2, 0:2], MK[:, n, :], ones[:, 0:2], start=(n == 0), stop=(n == NT - 1))
                last.then_inc(s_pos[l], 1)
                sh_down(0)
                sh_gate_up(2)
                pe.wait_ge(s_cb, l + 1)
                mm(PS[:, 2, 128:128 + E], cntB[:, :], before[0:E, 0:E], start=True, stop=True)
                mm(PS[:, 2, 128 + E:130 + E], cntB[:, :], ones[0:E, 0:2], start=True, stop=True).then_inc(s_ob, 1)
                sh_down(1)
                sh_gate_up(3)
                sh_down(2)
                sh_down(3)
                for i in range(NT * 8):
                    pe.wait_ge(s_pj[l], i + 1)
                    mm(PS[:, 0, 256:256 + 2 * NB], PJ[:, i % 4, :], RR[:, i % 4, :], start=(i == 0),
                       stop=(i == NT * 8 - 1)).then_inc(s_tb[l], 1)
                pe.wait_ge(s_tab[l], 2)
                pe.wait_ge(s_sye[l], 2 * NT)
                n = pe.value_load(extra[0:1, 0:1], min_val=0, max_val=OVER // 2) + E // 2

                def rows_T(b, s, it):
                    pe.wait_ge(s_ga[l][s], it * 16 + 16)
                    if isinstance(b, int) and b == 0:
                        pass
                    else:
                        pe.wait_ge(s_xl[l], b)
                    for k in range(KT):
                        last = nc.tensor.transpose(PS[:, k // 4, (k % 4) * P:(k % 4 + 1) * P],
                                                   XG[:, s, k * P:(k + 1) * P], ident[:, :])
                    last.then_inc(s_tx[l], 1)

                def gate_up(b, s):
                    pe.wait_ge(s_xl[l], b + 1)
                    pe.wait_ge(s_wl[l], b * 2 + 2)
                    if not (isinstance(b, int) and b < 2):
                        pe.wait_ge(s_hd[l], b - 1)
                    for k in range(KT):
                        xh, xl = XH[:, s, k * P:(k + 1) * P], XL[:, s, k * P:(k + 1) * P]
                        wh, wl = WH[:, s, :, k * F:(k + 1) * F], WL[s][:, :, k * F:(k + 1) * F]
                        for i, (a, w) in enumerate(((xh, wh), (xh, wl), (xl, wh))):
                            last = mm(PS[:, 3 + s, :].rearrange("p (a b) -> p a b", a=2), a, w,
                                      start=(k == 0 and i == 0), stop=(k == KT - 1 and i == 2))
                    last.then_inc(s_gu[l], 1)

                def hidden_T(b, s):
                    pe.wait_ge(s_hd[l], b + 1)
                    if not (isinstance(b, int) and b == 0):
                        pe.wait_ge(s_he[l], b)
                    for k in range(2):
                        last = nc.tensor.transpose(PS[:, 2, k * P:(k + 1) * P], Hm[:, s, k * P:(k + 1) * P], ident[:, :])
                    last.then_inc(s_ht[l], 1)

                def down_proj(b, s, it):
                    pe.wait_ge(s_he[l], b + 1)
                    pe.wait_ge(s_mw[l][3 * s + 2], it * 16 + 16)
                    if not (isinstance(b, int) and b == 0):
                        pe.wait_ge(s_ya[l], b)
                        pe.wait_ge(s_yv[l], b)
                    wd = W[:, 3 * s + 2, :].rearrange("p (k n) -> p k n", k=2)
                    for h in range(2):
                        for k in range(2):
                            last = mm(PS[:, 5 + h, :], HTm[:, s, k * P:(k + 1) * P], wd[:, k, h * 512:(h + 1) * 512],
                                      start=(k == 0), stop=(k == 1))
                    last.then_inc(s_yd[l], 1)

                def step(b, s, it, more):
                    hidden_T(b, s)
                    if more or s == 0:
                        gate_up(b + 1, 1 - s)
                    if more:
                        rows_T(b + 2, s, it + 1)
                    down_proj(b, s, it)

                rows_T(0, 0, 0)
                rows_T(1, 1, 0)
                gate_up(0, 0)
                step(0, 0, 0, True)
                step(1, 1, 0, True)
                with pe.Fori(1, n - 1) as it:
                    step(it * 2, 0, it, True)
                    step(it * 2 + 1, 1, it, True)
                step(n * 2 - 2, 0, n - 1, False)
                step(n * 2 - 1, 1, n - 1, False)

            pe.wait_ge(s_cst, 1)
            pe.wait_ge(s_vec, 16 * 5)
            nc.tensor.transpose(PS[:, 0, 0:40], vec_rows[:, :], ident[0:40, 0:40])
            for k in range(KT):
                last = nc.tensor.transpose(PS[:, 1, k * TAPS:(k + 1) * TAPS], DWR[:, k * P:(k + 1) * P], ident[0:TAPS, 0:TAPS])
            last.then_inc(s_vps, 1)
            for n in range(NT):
                x_T(n)
            pe.wait_ge(s_vev, 2)
            pe.wait_ge(s_xta, NT)
            pe.wait_ge(s_xtv, NT)
            for j in range(KT):
                m, c = j // 2, (j % 2) * P
                if j % 2 == 0:
                    landed(pe, ("a", m))
                    landed(pe, ("g", m))
                if j >= 2:
                    pe.wait_ge(s_h, j - 1)
                for key, bank in (("a", j % 2), ("g", 2 + j % 2)):
                    for k in range(KT):
                        last = mm(PS[:, bank, :], chunk((key, m))[:, k, c:c + P], XT[:, k, :], start=(k == 0), stop=(k == KT - 1))
                last.then_inc(s_ag, 1)
            for j in range(KT):
                pe.wait_ge(s_y, j + 1)
                last = mm(PS[:, 4, :], inv_d[:, :], Y[:, j, :], start=(j == 0), stop=(j == KT - 1))
            last.then_inc(s_mu, 1)
            for j in range(KT):
                pe.wait_ge(s_sq, j + 1)
                mm(PS[:, 5, :], inv_d[:, :], SQ[:, j % 2, :], start=(j == 0), stop=(j == KT - 1)).then_inc(s_vm, 1)
            pe.wait_ge(s_z, KT)
            out_proj(0, Y, "co")
            for n in range(NT):
                x_T(NT + n)
            moe(0)
            for n in range(NT):
                x_T(2 * NT + n)
            pe.wait_ge(s_xta, 3 * NT)
            pe.wait_ge(s_xtv, 3 * NT)
            for c in range(3 * 2 * NT):
                g, hf, n = c // 8, (c // 4) % 2, c % 4
                if n == 0:
                    landed(pe, ("v", g, 2 * hf))
                    landed(pe, ("v", g, 2 * hf + 1))
                if c == 8:
                    pe.wait_ge(s_xtp, KT)
                if c >= 4:
                    pe.wait_ge(s_ve if c % 2 == 0 else s_veh, (c - 4) // 2 + 1)
                src = XT if g == 0 else XTP
                for k in range(KT):
                    last = mm(PS[:, c % 4, :].rearrange("p (a b) -> p a b", a=2), src[:, k, n * P:(n + 1) * P],
                              pair(("v", g, 2 * hf), k), start=(k == 0), stop=(k == KT - 1))
                last.then_inc(s_v, 1)

            def items(u):
                return [(u, 0)] if u < 8 else [(8 + 2 * (u - 8), 1), (9 + 2 * (u - 8), 2)]

            def project(u):
                for i, g in items(u):
                    m, c = (u % 8) // 2, (u % 2) * P
                    for w, key in enumerate("qk"):
                        landed(pe, (key, g, m))
                        if i >= 1:
                            pe.wait_ge(s_qke, 2 * (i - 1) + w + 1)
                        for k in range(KT):
                            last = mm(PS[:, w, :], chunk((key, g, m))[:, k, c:c + P], XT[:, k, :], start=(k == 0),
                                      stop=(k == KT - 1))
                        last.then_inc(s_qk, 1)

            def scores(u):
                par = u % 2
                i = items(u)[-1][0]
                pe.wait_ge(s_rot, 2 * (i + 1))
                if u >= 1:
                    pe.wait_ge(s_p, 4 * u)
                for n in range(NT):
                    for half in range(2):
                        item = half if u >= 8 else 0
                        kn = n if (u >= 8 or half == 1 or n == 0) else n - 1
                        last = mm(PS[:, 2 + n // 2, (n % 2) * 256 + half * P:(n % 2) * 256 + (half + 1) * P],
                                  QT[:, par, item, n * P:(n + 1) * P], KTT[:, par, item, kn * P:(kn + 1) * P],
                                  start=True, stop=True)
                last.then_inc(s_s, 1)

            def probs_T(u):
                pe.wait_ge(s_p, 4 * u + 4)
                if u >= 1:
                    pe.wait_ge(s_pte, 2 * u)
                for n in range(NT):
                    for half in range(2):
                        c = 2 * n + half
                        last = nc.tensor.transpose(PS[:, 4 + c // 4, (c % 4) * P:(c % 4 + 1) * P],
                                                   PR[:, n, half * P:(half + 1) * P], ident[:, :])
                last.then_inc(s_pt, 1)

            def pv(u):
                h = u % 8
                pe.wait_ge(s_pte, 2 * u + 2)
                if u >= 1:
                    pe.wait_ge(s_oe, u)
                for n in range(NT):
                    for half in range(2):
                        g = 0 if u < 8 else 1 + half
                        kn = n if (u >= 8 or half == 1 or n == 0) else n - 1
                        last = mm(PS[:, 6, n * P:(n + 1) * P], PRT[:, 2 * n + half, :], V[:, g, kn, h * P:(h + 1) * P],
                                  start=(half == 0), stop=(half == 1))
                last.then_inc(s_o, 1)

            pe.wait_ge(s_ve, 3 * NT)
            pe.wait_ge(s_veh, 3 * NT)
            project(0)
            for u in range(16):
                if u < 15:
                    project(u + 1)
                if u >= 1:
                    probs_T(u - 1)
                scores(u)
                if u >= 1:
                    pv(u - 1)
            probs_T(15)
            pv(15)
            for c in range(2 * NT):
                o, n = (O0, O12)[c // NT], c % NT
                pe.wait_ge(s_wts, c + 1)
                if c >= 2:
                    pe.wait_ge(s_ote, 2 * (c - 1))
                for hf in range(2):
                    for h in range(4):
                        last = nc.tensor.transpose(PS[:, 4 + 2 * (c % 2) + hf, h * P:(h + 1) * P],
                                                   o[:, n, (4 * hf + h) * P:(4 * hf + h + 1) * P], ident[:, :])
                    last.then_inc(s_ot, 1)
            pe.wait_ge(s_ote, 4 * NT)
            out_proj(1, OT, "ao")
            for n in range(NT):
                x_T(3 * NT + n)
            moe(1)


_INS = ["x", "positions", "ln1_g", "ln1_b", "ln2_g", "ln2_b", "conv_w_in", "conv_b_in", "conv_w_dw", "conv_b_dw",
        "conv_ln_g", "conv_ln_b", "conv_w_out", "conv_b_out", "w_kv", "attn_w_q", "attn_w_o", "router_w",
        "router_bias", "exp_w_gate", "exp_w_up", "exp_w_down", "sh_w_gate", "sh_w_up", "sh_w_down"]


def kernel(**inputs):
    import concourse.bacc as bacc
    from concourse.bass_utils import run_bass_kernel_spmd

    nc = bacc.Bacc("TRN2", target_bir_lowering=False, num_devices=1)
    arrays, args = {}, []
    for name in _INS:
        a = np.ascontiguousarray(inputs[name])
        arrays[f"in_{name}"] = a
        args.append(nc.dram_tensor(f"in_{name}", a.shape, mybir.dt.from_np(a.dtype), kind="ExternalInput").ap())
    freq = np.float32(500000.0) ** (-np.arange(16, dtype=np.float32) * np.float32(2.0) / np.float32(32.0))
    arrays["inv_freq"] = np.concatenate([freq, freq]).astype(np.float32).reshape(32, 1)
    args.append(nc.dram_tensor("inv_freq", (32, 1), F32, kind="ExternalInput").ap())
    args.append(nc.dram_tensor("out", (1, T, D), F32, kind="ExternalOutput").ap())
    build(nc, *args)
    r = run_bass_kernel_spmd(nc, [arrays], core_ids=[0])
    return r.results[0]["out"]
```

```python
from contextlib import ExitStack

import numpy as np

import concourse.bass as bass
from concourse import mybir

F32 = mybir.dt.float32
I32 = mybir.dt.int32
U32 = mybir.dt.uint32
F32R = mybir.dt.float32r
ALU = mybir.AluOpType
ACT = mybir.ActivationFunctionType
AXX = mybir.AxisListType.X

P = 128
D = 1024
KT = D // P
T = 512
NT = T // P
TAPS = 31
POOL_TAPS = 11
HEADS = 8
QW = 3 * D
E = 64
F = 256
TOPK = 8
OVER = 32
NB = E + OVER
CH = 2048
SLOTS = 6
PIECES = 3
ALPHA = float(4.0 ** 0.25)
EPS = 1e-5
NEG = -1e30
QSCALE = float(128 ** -0.5)
ROUTED_SCALE = 2.5
MAGIC = 12582912.0
TWO_PI = (6.28125, 0.0019350051879882812, 3.0198280420415554e-07)
PI_LO = 3.1415925


def build(nc, x, positions, ln1_g, ln1_b, ln2_g, ln2_b, conv_w_in, conv_b_in, conv_w_dw, conv_b_dw,
          conv_ln_g, conv_ln_b, conv_w_out, conv_b_out, w_kv, attn_w_q, attn_w_o, router_w, router_bias,
          exp_w_gate, exp_w_up, exp_w_down, sh_w_gate, sh_w_up, sh_w_down, inv_freq, out):
    xrows = nc.dram_tensor("xrows", [T, D], F32, kind="Internal").ap()
    acc = nc.dram_tensor("acc", [T + P, D], F32, kind="Internal").ap()
    etab = nc.dram_tensor("etab", [2, NB], I32, kind="Internal").ap()
    stat_ex = nc.dram_tensor("stat_ex", [2, T, 2 * HEADS], F32, kind="Internal").ap()

    ctx = ExitStack()
    with ctx:
        def sb(name, shape, dt=F32):
            return ctx.enter_context(nc.sbuf_tensor(name, shape, dt))

        def sem(name):
            return ctx.enter_context(nc.semaphore(name))

        ident = sb("ident", [P, P])
        before = sb("before", [P, P])
        ones = sb("ones", [P, P])
        inv_d = sb("inv_d", [P, P])
        iota_f = sb("iota_f", [P, P])
        mask_near = sb("mask_near", [P, 256])
        mask_first = sb("mask_first", [P, 256])
        mask_far = sb("mask_far", [P, 256])
        imod = sb("imod", [P, P], I32)
        RW = sb("RW", [P, 2, KT, E])
        RB = sb("RB", [P, 2, E])
        LNG = sb("LNG", [P, D])
        LNB = sb("LNB", [P, D])
        cosT = sb("cosT", [32, T])
        sinT = sb("sinT", [32, T])
        vec_rows = sb("vec_rows", [40, P])
        vecT = sb("vecT", [P, 40])
        dwT = sb("dwT", [P, KT, TAPS])
        IDX = sb("IDX", [P, NB], U32)
        GTAB = sb("GTAB", [P, NB])
        IDXG = sb("IDXG", [P, 2], U32)
        IDXS = sb("IDXS", [P, 2], U32)
        base1 = sb("base1", [P, E])
        over_c = sb("over_c", [P, E])
        erow = sb("erow", [1, NB], I32)
        pcol = sb("pcol", [P, 8])
        sgn = sb("sgn", [32, 1])
        invf = sb("invf", [32, 1])
        eps = sb("eps", [P, 1])
        bns = sb("bns", [P, 2, 6])
        mv = sb("mv", [P, 2])
        rstd1 = sb("rstd1", [P, 1])
        std1 = sb("std1", [P, 1])
        scratch = sb("scratch", [P, 16])
        extra = sb("extra", [1, 1], I32)
        etmp = sb("etmp", [32, 2], I32)
        m8 = sb("m8", [P, NT, 8])
        s8 = sb("s8", [P, NT, 8])
        g8 = sb("g8", [P, NT, 8])
        s8i = sb("s8i", [P, NT * 8], I32)
        b8i = sb("b8i", [P, NT * 8], I32)
        p8i = sb("p8i", [P, NT * 8], I32)
        b8 = sb("b8", [P, NT * 8])
        p8 = sb("p8", [P, NT * 8])
        gsum = sb("gsum", [P, NT])
        grec = sb("grec", [P, NT])
        cnt = sb("cnt", [E, 4])
        cntB = sb("cntB", [E, P])
        obs = sb("obs", [P, E + 1])
        tabf = sb("tabf", [P, NB])
        delta = sb("delta", [P, E])
        statN = sb("statN", [P, 2, NT, 2 * HEADS])
        statP = sb("statP", [P, 2, NT, 2 * HEADS])
        wt = sb("wt", [P, 2, 4, NT, HEADS])
        mx = sb("mx", [P, NT])
        PS = ctx.enter_context(nc.psum_tensor("PS", [P, 8, 512], F32))

        def lay_out(layout):
            with ExitStack() as space:
                return [space.enter_context(nc.sbuf_tensor(name, [P] + shape, dt)) for name, shape, dt in layout]

        X, XT, BIG, W = lay_out([("X", [NT, D], F32),
                                 ("XT", [KT, T], F32),
                                 ("BIG", [23552], F32),
                                 ("W", [SLOTS, CH], F32)])
        WL0, WL1, WH, XL, _, XH = lay_out([("WL0", [2, CH], F32R), ("WL1", [2, CH], F32R), ("WH", [2, 2, CH], F32R),
                                           ("XL", [2, D], F32R), ("to_XH", [15616 - 10240], F32), ("XH", [2, D], F32R)])
        WL = (WL0, WL1)
        _, XTH, _, RAW, PH, PL, XTL = lay_out([("to_XTH", [NT, D], F32), ("XTH", [KT, T], F32R), ("to_RAW", [23552], F32),
                                               ("RAW", [PIECES, D], F32), ("PH", [PIECES, D], F32R),
                                               ("PL", [PIECES, D], F32R), ("XTL", [KT, T], F32R)])
        sb("all_layouts", [P, 2 * NT * D + 23552 + 3 * PIECES * D + KT * T])

        def big(at, *shape):
            n = int(np.prod(shape))
            ap = BIG[:, at:at + n]
            if len(shape) == 2:
                return ap.rearrange("p (a b) -> p a b", a=shape[0])
            if len(shape) == 3:
                return ap.rearrange("p (a b c) -> p a b c", a=shape[0], b=shape[1])
            return ap

        HALO = TAPS - 1
        HP = big(0, KT, HALO + T)
        Y = big(4352, KT, T)
        SG = big(8448, 2, T)
        SQ = big(9472, 2, T)
        RS = big(10496, T)
        DWR = BIG[0:TAPS, 11008:11008 + D]
        ROT = BIG[0:32, 16384:16384 + 4 * T].rearrange("p (a b) -> p a b", a=4)
        POSI = BIG[0:32, 18432:18432 + T]
        BOUT = big(15360, D)
        TP = big(18944, 4, T)
        Y2 = big(20992, 4, T)
        V = BIG[:, 0:12288].rearrange("p (g n c) -> p g n c", g=3, n=NT)
        O0 = big(12288, NT, D)
        O12 = big(0, NT, D)
        QT = big(16384, 2, 2, T)
        KTT = big(18432, 2, 2, T)
        PR = big(20480, NT, 256)
        PRT = big(21504, 8, P)
        RT = BIG[0:32, 22528:22528 + 2 * T].rearrange("p (a b) -> p a b", a=2)
        OT = big(4096, HEADS, T)
        SC, BI, BR, MK, GS, GT, SLM = (big(256 * i, NT, E) for i in range(7))
        EQ = BIG[:, 2048:4096].rearrange("p (n j e) -> p n j e", n=NT, j=8)
        EG = BIG[:, 4096:6144].rearrange("p (n j e) -> p n j e", n=NT, j=8)
        SLs = big(7424, 2, F)
        UPs = big(7936, 2, F)
        HSs = big(8448, 2, F)
        HTs = big(8960, 2, F)
        YS = big(9472, 2, D)
        AXB = big(11520, 2, D)
        XG = big(13568, 2, D)
        YB = big(17664, 2, D)
        PJ = BIG[:, 17664:19712].rearrange("p (s j q) -> p s j q", s=2, j=8)
        RR = BIG[:, 19712:22784].rearrange("p (s j b) -> p s j b", s=2, j=8)
        SLm = big(19712, 2, F)
        Hm = big(20224, 2, F)
        HTm = big(20736, 2, F)

        s_vec, s_posd, s_zero, s_etab0 = sem("vec_loaded"), sem("pos_loaded"), sem("zeros_stored"), sem("etab_head")
        s_xin = [sem(f"x_loaded{n}") for n in range(NT)]
        s_rw = sem("router_loaded")
        s_gb = sem("ln_vectors_loaded")
        s_w = [sem(f"chunk{i}_loaded") for i in range(SLOTS)]
        s_cst = sem("constants_ready")
        s_pool = sem("pool_chain")
        s_dve = sem("dve_chain")
        s_act = sem("act_chain")
        s_vps, s_vev = sem("vectors_transposed"), sem("vectors_copied")
        s_ang, s_trig = sem("angles_ready"), sem("sines_ready")
        s_xps, s_xta, s_xtv = sem("x_transposed"), sem("xt_low_copied"), sem("xt_high_copied")
        s_ag, s_sg, s_h, s_y = sem("glu_products"), sem("glu_sigmoid"), sem("glu_out"), sem("conv_out")
        s_yp, s_tp = sem("conv_first_taps"), sem("tap_products")
        s_mu, s_yc, s_sq, s_vm = sem("mean_ready"), sem("centred"), sem("squared"), sem("variance_steps")
        s_std, s_t, s_z = sem("conv_std"), sem("conv_normed"), sem("conv_silu")
        s_mix = [sem(f"mix{i}_product") for i in range(2)]
        s_res = sem("residual_added")
        s_nvar, s_nstd, s_norm = sem("norm_variance"), sem("norm_std"), sem("norm_out")
        s_xr = [sem(f"xrows_stored{i}") for i in range(2)]
        s_rt = sem("router_logits")
        s_sc = sem("router_scores")
        s_mk = sem("router_mask")
        s_pos = sem("ranks_ready")
        s_cb = sem("counts_spread")
        s_ob = sem("overflow_bases")
        s_pj = [sem(f"onehots{i}") for i in range(2)]
        s_tb = [sem(f"table_steps{i}") for i in range(2)]
        s_tab = sem("tables_ready")
        s_et = [sem(f"etab_stored{i}") for i in range(2)]
        s_sgu = [sem(f"shared_gate_up{i}") for i in range(2)]
        s_ssl = [sem(f"shared_silu{i}") for i in range(2)]
        s_sh = [sem(f"shared_hidden{i}") for i in range(2)]
        s_sht = [sem(f"shared_hidden_T{i}") for i in range(2)]
        s_she = [sem(f"shared_hidden_T_copied{i}") for i in range(2)]
        s_sy = [sem(f"shared_product{i}") for i in range(2)]
        s_sye = [sem(f"shared_out{i}") for i in range(2)]
        s_ax = [sem("acc_low_tile"), sem("acc_high_tile")]
        s_acc = [[sem(f"acc_stored{i}_{k}") for k in range(2)] for i in range(2)]
        s_xg0 = [sem(f"gather_cleared{i}") for i in range(2)]
        s_mw = [[sem(f"expert_w{i}_{k}") for k in range(SLOTS)] for i in range(2)]
        s_ga = [[sem(f"gathered{i}_{k}") for k in range(2)] for i in range(2)]
        s_tx = [sem(f"gather_transposed{i}") for i in range(2)]
        s_xh = [sem(f"rows_high{i}") for i in range(2)]
        s_xl = [sem(f"rows_low{i}") for i in range(2)]
        s_wh = [sem(f"weights_high{i}") for i in range(2)]
        s_wl = [sem(f"weights_low{i}") for i in range(2)]
        s_gu = [sem(f"gate_up{i}") for i in range(2)]
        s_sl = [sem(f"expert_silu{i}") for i in range(2)]
        s_hd = [sem(f"expert_hidden{i}") for i in range(2)]
        s_ht = [sem(f"hidden_transposed{i}") for i in range(2)]
        s_he = [sem(f"hidden_T_copied{i}") for i in range(2)]
        s_yd = [sem(f"expert_out{i}") for i in range(2)]
        s_ya = [sem(f"expert_out_low_copied{i}") for i in range(2)]
        s_yv = [sem(f"expert_out_high_copied{i}") for i in range(2)]
        s_scat = [sem(f"scattered{i}") for i in range(2)]
        s_ph, s_pl = sem("piece_high"), sem("piece_low")
        s_v, s_ve = sem("v_product"), sem("v_copied")
        s_qk, s_qke, s_rot, s_rots = sem("qk_product"), sem("qk_copied"), sem("qk_rotated"), sem("qk_shuffled")
        s_s, s_m, s_p = sem("scores_ready"), sem("row_max_ready"), sem("probs_ready")
        s_pt, s_pte = sem("probs_transposed"), sem("probs_T_copied")
        s_o, s_oe = sem("pv_product"), sem("pv_copied")
        s_st0, s_st1 = sem("stats_out"), sem("stats_in")
        s_ic = [sem(f"indices_copied{i}") for i in range(2)]
        s_go = sem("indirect_dmas_released")
        s_veh = sem("v_copied_odd")
        s_dve_w = sem("mix_exponents")
        s_wexp, s_wts = sem("mix_exp"), sem("mix_weighted")
        s_ot, s_otn, s_ote = sem("heads_transposed"), sem("near_heads_T_copied"), sem("far_heads_T_added")
        s_out = sem("out_stored")

        chunks = {}

        def wide(src, c):
            return src[:, c * F:(c + 1) * F].rearrange("(k p) n -> p k n", p=P)

        def down(src):
            return src.rearrange("(k p) n -> p k n", p=P)

        order = []
        for m in range(4):
            order += [(("a", m), wide(conv_w_in[0], m), 8, (s_ag, 2 * m + 2)),
                      (("g", m), wide(conv_w_in[0], 4 + m), 8, (s_ag, 2 * m + 2))]
        order += [(("co", m), wide(conv_w_out[0], m), 8, (s_mix[0], NT)) for m in range(4)]

        def shared(l):
            return [(("sg", l), wide(sh_w_gate[l], 0), 8, (s_sgu[l], NT)),
                    (("su", l), wide(sh_w_up[l], 0), 8, (s_sgu[l], NT)),
                    (("sd", l), down(sh_w_down[l]), 2, (s_sy[l], 2 * NT))]

        order += shared(0)
        n_first = len(order)
        order += [(("ao", m), wide(attn_w_o[0], m), 8, (s_mix[1], NT)) for m in range(4)]
        order += shared(1)
        count = [0] * SLOTS
        owner = [None] * SLOTS
        plan, pieces = [], []
        for i, (key, src, k, freed) in enumerate(order):
            if i == n_first:
                freed_first = list(owner)
                for g in range(3):
                    for hf in range(2):
                        at = QW + g * D + hf * 512
                        pieces += [w_kv[2 * P * q:2 * P * (q + 1), at:at + 512].rearrange("(k p) n -> p k n", p=P)
                                   for q in range(4)]
                for h, g in [(h, 0) for h in range(HEADS)] + [(h, g) for h in range(HEADS) for g in (1, 2)]:
                    at = g * D + h * P
                    pieces += [w[:, at:at + P].rearrange("(k p) n -> p k n", p=P) for w in (attn_w_q[0], w_kv)]
                piece_at = []
                for j in range(len(pieces)):
                    count[j % PIECES] += 1
                    piece_at.append((s_w[j % PIECES], 16 * count[j % PIECES]))
                owner = [(s_pl, len(pieces))] + [(s_qk, 2 * 3 * HEADS)] * 5
            slot = (i if i < n_first else i - n_first) % SLOTS
            if key == ("sd", 1):
                slot = 2
            count[slot] += 1
            plan.append((key, src, k, slot, owner[slot]))
            chunks[key] = (slot, 16 * count[slot])
            owner[slot] = freed
        n_v = 3 * 2 * 4

        def piece_used(j):
            return (s_v, j + 1) if j < n_v else (s_qk, j - n_v + 1)

        freed_last = list(owner)

        def chunk(key, k=8):
            return W[:, chunks[key][0], :].rearrange("p (k n) -> p k n", k=k)

        def landed(eng, key):
            slot, value = chunks[key]
            eng.wait_ge(s_w[slot], value)

        def pair(key, k):
            s = chunks[key][0]
            return W[:, s:s + 2, k * F:(k + 1) * F]

        block = ctx.enter_context(nc.Block())

        @block.sync
        def _(sp):
            def load_chunk(i):
                key, src, k, slot, freed = plan[i]
                if freed is not None:
                    sp.wait_ge(*freed)
                sp.dma_start(W[:, slot, :].rearrange("p (k n) -> p k n", k=k), src).then_inc(s_w[slot], 16)

            def ln_vectors(r):
                if r:
                    sp.wait_ge(s_norm, NT * r)
                g, b = (ln1_g, ln1_b) if r % 2 == 0 else (ln2_g, ln2_b)
                sp.dma_start(LNG[:, :], g[r // 2:r // 2 + 1, :].broadcast_to([P, D])).then_inc(s_gb, 16)
                sp.dma_start(LNB[:, :], b[r // 2:r // 2 + 1, :].broadcast_to([P, D])).then_inc(s_gb, 16)

            def store_xrows(l):
                for n in range(NT):
                    sp.wait_ge(s_norm, 2 * NT * l + n + 1)
                    sp.dma_start(xrows[n * P:(n + 1) * P, :], X[:, n, :]).then_inc(s_xr[l], 16)

            def moe(l):
                freed = freed_first if l == 0 else freed_last

                def load(slot, e):
                    s, c = slot // 3, slot % 3
                    if c < 2:
                        src = (exp_w_gate, exp_w_up)[c][l, bass.ds(e, 1)].rearrange("e (p k) n -> p (e k) n", p=P)
                        dst = W[:, slot, :].rearrange("p (k n) -> p k n", k=KT)
                    else:
                        src = exp_w_down[l, bass.ds(e, 1)].rearrange("e (k p) n -> p (e k) n", p=P)
                        dst = W[:, slot, :].rearrange("p (k n) -> p k n", k=2)
                    sp.dma_start(dst, src).then_inc(s_mw[l][slot], 16)

                def store_acc(n):
                    sp.wait_ge(s_ax[n // 2], 2 * l + n % 2 + 1)
                    sp.dma_start(acc[n * P:(n + 1) * P, :], AXB[:, n % 2, :]).then_inc(s_acc[l][n % 2], 16)

                for used in (s_mix[l], s_sgu[l], s_sy[l]):
                    for slot in range(SLOTS):
                        if freed[slot][0] is used:
                            sp.wait_ge(*freed[slot])
                            load(slot, slot // 3)
                    if used is s_mix[l]:
                        store_acc(0)
                        store_acc(1)
                store_acc(2)
                store_acc(3)
                sp.wait_ge(s_tab, 2 * l + 2)
                sp.dma_start(etab[l, E:NB].rearrange("(a b) -> a b", b=1), etmp[:, 1:2]).then_inc(s_et[l], 16)
                sp.wait_ge(s_et[l], 16)
                n = sp.value_load(extra[0:1, 0:1], min_val=0, max_val=OVER // 2) + E // 2

                def load_gate_up(b, s):
                    e = sp.value_load(etab[l:l + 1, bass.ds(b, 1)], min_val=0, max_val=E - 1)
                    for c in range(2):
                        sp.wait_ge(s_wl[l], b * 2 - 3 + c)
                        load(3 * s + c, e)

                def load_down(b, s):
                    e = sp.value_load(etab[l:l + 1, bass.ds(b, 1)], min_val=0, max_val=E - 1)
                    sp.wait_ge(s_yd[l], b - 1)
                    load(3 * s + 2, e)

                load_gate_up(2, 0)
                with sp.Fori(0, n - 2) as it:
                    load_gate_up(it * 2 + 3, 1)
                    load_down(it * 2 + 2, 0)
                    load_gate_up(it * 2 + 4, 0)
                    load_down(it * 2 + 3, 1)
                load_gate_up(n * 2 - 1, 1)
                load_down(n * 2 - 2, 0)
                load_down(n * 2 - 1, 1)
                for t in range(NT):
                    if t == 0:
                        sp.wait_ge(s_scat[l], n * 32)
                    sp.dma_start(X[:, t, :], acc[t * P:(t + 1) * P, :]).then_inc(s_xin[t], 16)
                return n

            for row, (v, k) in enumerate(((conv_b_in, 16), (conv_b_dw, 8), (conv_ln_g, 8), (conv_ln_b, 8))):
                at = (0, 16, 24, 32)[row]
                sp.dma_start(vec_rows[at:at + k, :], v.rearrange("a (k p) -> (a k) p", p=P)).then_inc(s_vec, 16)
            sp.dma_start(DWR, conv_w_dw[0]).then_inc(s_vec, 16)
            for n in range(NT):
                sp.dma_start(X[:, n, :], x[0, n * P:(n + 1) * P, :]).then_inc(s_xin[n], 16)
            load_chunk(0)
            load_chunk(1)
            sp.dma_start(POSI.bitcast(I32), positions.broadcast_to([32, T])).then_inc(s_posd, 16)
            sp.dma_start(invf[:, :], inv_freq).then_inc(s_posd, 16)
            for i in range(2, 6):
                load_chunk(i)
            sp.dma_start(BOUT, conv_b_out.broadcast_to([P, D])).then_inc(s_gb, 16)
            ln_vectors(0)
            for l in range(2):
                sp.dma_start(RW[:, l, :, :], router_w[l].rearrange("(k p) e -> p k e", p=P)).then_inc(s_rw, 16)
                sp.dma_start(RB[:, l, :], router_bias[l:l + 1, :].broadcast_to([P, E])).then_inc(s_rw, 16)
            sp.wait_ge(s_cst, 1)
            sp.dma_start(acc[T:T + P, :], XG[:, 0, :]).then_inc(s_zero, 16)
            for l in range(2):
                sp.dma_start(etab[l:l + 1, :], erow[:, :]).then_inc(s_etab0, 16)
            for i in range(6, n_first):
                load_chunk(i)
            store_xrows(0)
            ln_vectors(1)
            sp.wait_ge(s_etab0, 32)
            n0 = moe(0)
            sp.wait_ge(s_yd[0], n0 * 2)
            for j, src in enumerate(pieces):
                if j == PIECES:
                    ln_vectors(2)
                if j >= PIECES:
                    sp.wait_ge(s_pl, j - PIECES + 1)
                sp.dma_start(RAW[:, j % PIECES, :].rearrange("p (k n) -> p k n", k=src.shape[1]), src).then_inc(piece_at[j][0], 16)
            for i in range(n_first, n_first + SLOTS):
                load_chunk(i)
            sp.wait_ge(s_p, 4 * 16)
            sp.wait_ge(s_m, 16)
            sp.dma_start(stat_ex[0].rearrange("(n p) c -> p n c", p=P), statN[:, 0, :, :]).then_inc(s_st0, 16)
            sp.dma_start(stat_ex[1].rearrange("(i j) c -> i j c", j=NT), statP[:, 1, :, :]).then_inc(s_st0, 16)
            sp.wait_ge(s_st0, 32)
            sp.dma_start(statP[:, 0, :, :], stat_ex[0].rearrange("(i j) c -> i j c", j=NT)).then_inc(s_st1, 16)
            sp.dma_start(statN[:, 1, :, :], stat_ex[1].rearrange("(n p) c -> p n c", p=P)).then_inc(s_st1, 16)
            for i in range(n_first + SLOTS, len(plan)):
                load_chunk(i)
            store_xrows(1)
            ln_vectors(3)
            moe(1)
            for n in range(NT):
                sp.wait_ge(s_norm, 3 * NT + n + 1)
                sp.dma_start(out[0, n * P:(n + 1) * P, :], X[:, n, :]).then_inc(s_out, 16)
            sp.wait_ge(s_out, 16 * NT)
            sp.wait_ge(s_zero, 16)

        @block.gpsimd
        def _(pool):
            chain = [0]

            def link(ins):
                chain[0] += 1
                ins.then_inc(s_pool, 1)
                pool.wait_ge(s_pool, chain[0])

            pool.memset(XG[:, 0, :], 0.0)
            pool.memset(ones[:, :], 1.0)
            pool.memset(inv_d[:, :], 1.0 / D)
            pool.memset(eps[:, :], EPS)
            pool.memset(HP[:, :, 0:HALO], 0.0)
            pool.iota(erow[:, :], [[1, NB]], base=0, channel_multiplier=0)
            pool.memset(ident[:, :], 0.0)
            pool.memset(mask_near[:, :], 0.0)
            pool.memset(mask_first[:, :], 0.0)
            pool.memset(sgn[:, :], 1.0)
            pool.iota(iota_f[:, :], [[1, P]], base=0, channel_multiplier=0, allow_small_or_imprecise_dtypes=True)
            pool.iota(pcol[:, 0:1], [[0, 1]], base=0, channel_multiplier=1, allow_small_or_imprecise_dtypes=True)
            pool.iota(pcol[:, 1:2], [[0, 1]], base=T + 1, channel_multiplier=1, allow_small_or_imprecise_dtypes=True)
            pool.iota(pcol[:, 2:2 + NT], [[P, NT]], base=1, channel_multiplier=1, allow_small_or_imprecise_dtypes=True)
            pool.iota(base1[:, :], [[P, E]], base=1, channel_multiplier=0, allow_small_or_imprecise_dtypes=True)
            pool.iota(over_c[:, :], [[-P, E]], base=P * (E - 1), channel_multiplier=0, allow_small_or_imprecise_dtypes=True)
            link(pool.iota(imod[:, :], [[-1, P]], base=P, channel_multiplier=1))
            pool.affine_select(out=ident[:, :], in_=ident[:, :], compare_op=ALU.not_equal, fill=1.0, base=0,
                               pattern=[[-1, P]], channel_multiplier=1)
            pool.affine_select(out=before[:, :], in_=ones[:, :], compare_op=ALU.is_gt, fill=0.0, base=0,
                               pattern=[[1, P]], channel_multiplier=-1)
            pool.affine_select(out=sgn[:, :], in_=sgn[:, :], compare_op=ALU.is_ge, fill=-1.0, base=-16,
                               pattern=[[0, 1]], channel_multiplier=1)
            pool.affine_select(out=mask_near[:, 0:P], in_=mask_near[:, 0:P], compare_op=ALU.is_ge, fill=NEG, base=0,
                               pattern=[[1, P]], channel_multiplier=-1)
            for m in (mask_near, mask_first):
                last = pool.affine_select(out=m[:, P:256], in_=m[:, P:256], compare_op=ALU.is_ge, fill=NEG, base=0,
                                          pattern=[[-1, P]], channel_multiplier=1)
            link(last)
            link(pool.memset(mask_first[:, 0:P], NEG))
            pool.memset(mask_far[:, 0:P], 0.0).then_inc(s_cst, 1)
            pool.wait_ge(s_cst, 1)
            pool.wait_ge(s_ang, 1)
            for h in range(2):
                pool.affine_select(out=mask_far[:, h * P:(h + 1) * P], in_=mask_far[:, h * P:(h + 1) * P],
                                   compare_op=ALU.is_ge, fill=NEG, base=0, pattern=[[-1, P]],
                                   channel_multiplier=1).then_inc(s_cst, 1)

            for j in range(KT):
                for w in range(1, POOL_TAPS):
                    i = j * POOL_TAPS + w
                    pool.wait_ge(s_tp, i + 1)
                    pool.tensor_tensor(Y[:, j, :], Y[:, j, :], TP[:, i % 4, :], ALU.add).then_inc(s_yp, 1)
                    pool.wait_ge(s_yp, j * (POOL_TAPS - 1) + w)

            def moe(l):
                pool.wait_ge(s_norm, 2 * NT * l + NT)
                pool.wait_ge(s_zero, 16)
                link(pool.memset(XG[:, 0:2, :], 0.0))
                for n in range(NT):
                    pool.wait_ge(s_ssl[l], 2 * n + 2)
                    if n >= 2:
                        pool.wait_ge(s_sht[l], n - 1)
                    pool.tensor_tensor(HSs[:, n % 2, :], SLs[:, n % 2, :], UPs[:, n % 2, :], ALU.mult).then_inc(s_sh[l], 1)
                    if n in (1, 2):
                        mix_in(l, n - 1)
                pool.wait_ge(s_tab, 2 * l + 2)
                pool.wait_ge(s_xr[l], 16 * NT)
                n = pool.value_load(extra[0:1, 0:1], min_val=0, max_val=OVER // 2) + E // 2

                def some_slots(b):
                    return [pool.value_load(IDX[i:i + 1, bass.ds(b, 1)].bitcast(I32), min_val=0, max_val=T + P)
                            for i in (48, 64, 80, 96)]

                def by_size(slots, rows):
                    slot48, slot64, slot80, slot96 = slots
                    with pool.If(slot64 < T):
                        with pool.If(slot96 < T):
                            rows(P)
                        with pool.Else():
                            with pool.If(slot80 < T):
                                rows(96)
                            with pool.Else():
                                rows(80)
                            pool.sem_inc(s_go, 1)
                        pool.sem_inc(s_go, 1)
                    with pool.Else():
                        with pool.If(slot48 < T):
                            rows(64)
                        with pool.Else():
                            rows(48)
                        pool.sem_inc(s_go, 1)

                def gather(b, s):
                    slots = some_slots(b)
                    pool.tensor_copy(IDXG[:, s:s + 1], IDX[:, bass.ds(b, 1)]).then_inc(s_ic[l], 1)
                    pool.wait_ge(s_ic[l], b + 1 if isinstance(b, int) and b < 3 else b * 2 - 2)
                    pool.sem_inc(s_go, 1)

                    def rows(r):
                        pool.indirect_dma_start(XG[0:r, s, :], None, xrows,
                                                bass.IndirectOffsetOnAxis(IDXG[0:r, s:s + 1], axis=0),
                                                bounds_check=T - 1, oob_is_err=False).then_inc(s_ga[l][s], 16)

                    by_size(slots, rows)

                def scatter(b, s, copies):
                    slots = some_slots(b)
                    pool.tensor_copy(IDXS[:, s:s + 1], IDX[:, bass.ds(b, 1)]).then_inc(s_ic[l], 1)
                    pool.wait_ge(s_ic[l], copies)
                    pool.wait_ge(s_ya[l], b + 1)
                    pool.wait_ge(s_yv[l], b + 1)
                    if not (isinstance(b, int) and b == 0):
                        pool.wait_ge(s_scat[l], b * 16)
                    pool.sem_inc(s_go, 1)

                    def rows(r):
                        pool.indirect_dma_start(acc, bass.IndirectOffsetOnAxis(IDXS[0:r, s:s + 1], axis=0), YB[0:r, s, :],
                                                None, compute_op=ALU.add).then_inc(s_scat[l], 16)

                    by_size(slots, rows)

                gather(0, 0)
                gather(1, 1)
                pool.wait_ge(s_tx[l], 1)
                gather(2, 0)
                for k in range(2):
                    pool.wait_ge(s_acc[l][k], 16 * NT // 2)

                def step(b, s):
                    pool.wait_ge(s_tx[l], b + 2)
                    gather(b + 3, 1 - s)
                    scatter(b, s, b * 2 + 5)

                step(0, 0)
                step(1, 1)
                with pool.Fori(1, n - 2) as it:
                    step(it * 2, 0)
                    step(it * 2 + 1, 1)
                step(n * 2 - 4, 0)
                for k in range(3):
                    scatter(n * 2 - 3 + k, (1 + k) % 2, n * 4 - 2 + k)

            def mix_in(l, n):
                link(pool.tensor_scalar(AXB[:, n % 2, :], X[:, n, :], ALPHA, None, ALU.mult))
                pool.wait_ge(s_sye[l], 2 * n + 2)
                pool.tensor_tensor(AXB[:, n % 2, :], AXB[:, n % 2, :], YS[:, n % 2, :], ALU.add).then_inc(s_ax[0], 1)

            moe(0)
            moe(1)

        @block.scalar
        def _(act):
            A = nc.scalar.activation

            def xt_low(q):
                n = q % NT
                act.wait_ge(s_xps, q + 1)
                if q // NT == 2:
                    A(XTH[:, :, n * P:(n + 1) * P], PS[:, 4 + 2 * (n % 2):6 + 2 * (n % 2), :].rearrange("p a (k t) -> p (a k) t", k=4),
                      ACT.Copy).then_inc(s_xta, 1)
                    return
                A(XT[:, 0:4, n * P:(n + 1) * P], PS[:, 4 + 2 * (n % 2), :].rearrange("p (k t) -> p k t", k=4),
                  ACT.Copy).then_inc(s_xta, 1)

            def norm_round(r):
                for n in range(NT):
                    act.wait_ge(s_nvar, NT * r + n + 1)
                    A(std1[:, :], mv[:, 1:2], ACT.Sqrt, bias=eps[:, :]).then_inc(s_nstd, 1)
                    if r < 3:
                        if n >= 1:
                            xt_low(NT * (r + 1) + n - 1)
                if r < 3:
                    xt_low(NT * (r + 1) + NT - 1)

            def moe(l):
                act.wait_ge(s_norm, 2 * NT * l + NT)
                act.wait_ge(s_rt, l + 1)
                A(SC, PS[:, 0, 0:256].rearrange("p (n e) -> p n e", n=NT), ACT.Sigmoid).then_inc(s_sc, 1)
                for n in range(NT + 1):
                    if n < NT:
                        act.wait_ge(s_sgu[l], n + 1)
                        if n >= 2:
                            act.wait_ge(s_sh[l], n - 1)
                        A(SLs[:, n % 2, :], PS[:, 4 + n % 2, 0:F], ACT.Silu).then_inc(s_ssl[l], 1)
                        A(UPs[:, n % 2, :], PS[:, 4 + n % 2, F:2 * F], ACT.Copy).then_inc(s_ssl[l], 1)
                    if n >= 1:
                        m = n - 1
                        act.wait_ge(s_sht[l], m + 1)
                        if m >= 2:
                            act.wait_ge(s_sy[l], 2 * (m - 1))
                        A(HTs[:, m % 2, :], PS[:, 6, 0:F], ACT.Copy).then_inc(s_she[l], 1)
                        for h in range(2):
                            act.wait_ge(s_sy[l], 2 * m + h + 1)
                            if m >= 2 and h == 0:
                                act.wait_ge(s_ax[0], 2 * l + m - 1)
                            A(YS[:, m % 2, h * 512:(h + 1) * 512], PS[:, 7 if h == 0 else 3, :], ACT.Copy).then_inc(s_sye[l], 1)
                act.wait_ge(s_tab, 2 * l + 2)
                n = act.value_load(extra[0:1, 0:1], min_val=0, max_val=OVER // 2) + E // 2

                act.wait_ge(s_ax[1], 2 * l + 2)
                act.wait_ge(s_xr[l], 16 * NT)

                def rows_high(b, s):
                    act.wait_ge(s_tx[l], b + 1)
                    A(XH[:, s, :], PS[:, 0:2, :].rearrange("p a t -> p (a t)"), ACT.Copy).then_inc(s_xh[l], 1)

                def weights_high(b, s, it):
                    for c in range(2):
                        act.wait_ge(s_mw[l][3 * s + c], it * 16 + 16)
                        A(WH[:, s, c, :], W[:, 3 * s + c, :], ACT.Copy).then_inc(s_wh[l], 1)

                def silu(b, s):
                    act.wait_ge(s_gu[l], b + 1)
                    A(SLm[:, s, :], PS[:, 3 + s, 0:F], ACT.Silu).then_inc(s_sl[l], 1)

                def out_low(b, s):
                    act.wait_ge(s_yd[l], b + 1)
                    if not (isinstance(b, int) and b < 2):
                        act.wait_ge(s_scat[l], (b - 1) * 16)
                    A(YB[:, s, 0:512], PS[:, 5, :], ACT.Copy).then_inc(s_ya[l], 1)

                def step(b, s, it, more):
                    if more:
                        weights_high(b + 2, s, it + 1)
                    if more or s == 0:
                        silu(b + 1, 1 - s)
                    if more:
                        rows_high(b + 2, s)
                    out_low(b, s)

                for s in range(2):
                    rows_high(s, s)
                    weights_high(s, s, 0)
                silu(0, 0)
                step(0, 0, 0, True)
                step(1, 1, 0, True)
                with act.Fori(1, n - 1) as it:
                    step(it * 2, 0, it, True)
                    step(it * 2 + 1, 1, it, True)
                step(n * 2 - 2, 0, None, False)
                step(n * 2 - 1, 1, None, False)

            act.wait_ge(s_vps, 1)
            A(vecT[:, :], PS[:, 0, 0:40], ACT.Copy).then_inc(s_vev, 1)
            A(dwT[:, :, :], PS[:, 1, 0:KT * TAPS].rearrange("p (k t) -> p k t", k=KT), ACT.Copy).then_inc(s_vev, 1)
            for n in range(NT):
                xt_low(n)
            act.wait_ge(s_vev, 2)
            for j in range(KT):
                act.wait_ge(s_ag, j + 1)
                if j >= 2:
                    act.wait_ge(s_h, j - 1)
                A(SG[:, j % 2, :], PS[:, 2 + j % 2, :], ACT.Sigmoid, bias=vecT[:, 8 + j:9 + j]).then_inc(s_sg, 1)
                act.wait_ge(s_h, j + 1)
                for w in range(POOL_TAPS):
                    i = j * POOL_TAPS + w
                    tap, weight = HP[:, j, w:w + T], dwT[:, j, w:w + 1]
                    if w == 0:
                        A(Y[:, j, :], tap, ACT.Identity, scale=weight, bias=vecT[:, 16 + j:17 + j]).then_inc(s_tp, 1)
                        continue
                    before4 = i - 4 if (i - 4) % POOL_TAPS else i - 5
                    if before4 > 0:
                        act.wait_ge(s_yp, before4 - before4 // POOL_TAPS)
                    A(TP[:, i % 4, :], tap, ACT.Copy, scale=weight).then_inc(s_tp, 1)
            act.wait_ge(s_ang, 3)
            A(sinT[:, :], ROT[:, 0, :], ACT.Sin).then_inc(s_trig, 1)
            A(cosT[:, :], ROT[:, 1, :], ACT.Sin).then_inc(s_trig, 1)
            for j in range(KT):
                act.wait_ge(s_yc, j + 1)
                if j >= 2:
                    act.wait_ge(s_vm, j - 1)
                A(SQ[:, j % 2, :], Y[:, j, :], ACT.Square).then_inc(s_sq, 1)
            act.wait_ge(s_vm, KT)
            A(RS, PS[:, 5, :], ACT.Sqrt, bias=eps[:, :]).then_inc(s_std, 1)
            for j in range(KT):
                act.wait_ge(s_t, j + 1)
                A(Y[:, j, :], Y[:, j, :], ACT.Silu, scale=vecT[:, 24 + j:25 + j], bias=vecT[:, 32 + j:33 + j]).then_inc(s_z, 1)
            norm_round(0)
            moe(0)
            norm_round(1)

            def piece_high(j):
                if j >= len(pieces):
                    return
                act.wait_ge(*piece_at[j])
                if j >= PIECES:
                    act.wait_ge(*piece_used(j - PIECES))
                A(PH[:, j % PIECES, :], RAW[:, j % PIECES, :], ACT.Copy).then_inc(s_ph, 1)

            for j in range(PIECES - 1):
                piece_high(j)
            for j in range(n_v):
                piece_high(j + PIECES - 1)
                if j % 4 == 3:
                    act.wait_ge(s_v, j + 1)
                    c = j // 4
                    for n in (0, 2):
                        A(V[:, c // 2, n, (c % 2) * 512:(c % 2 + 1) * 512], PS[:, 4 * (c % 2) + n, :], ACT.Copy).then_inc(s_ve, 1)

            def qk_copy(i, g, par, item):
                for w, dst in enumerate((QT, KTT)):
                    piece_high(n_v + 2 * i + w + PIECES - 1)
                    act.wait_ge(s_qk, 2 * i + w + 1)
                    o = dst[:, par, item, :]
                    if g == 0:
                        A(o, PS[:, w, :], ACT.Copy).then_inc(s_qke, 1)
                    else:
                        A(o.rearrange("p (j i) -> p j i", j=NT), PS[:, w, :].rearrange("p (i j) -> p j i", j=NT),
                          ACT.Copy).then_inc(s_qke, 1)

            def softmax(u):
                st = statN[:, 0] if u < 8 else statP[:, 1]
                h = u % 8
                act.wait_ge(s_m, u + 1)
                if u >= 1:
                    act.wait_ge(s_pt, u)
                for n in range(NT):
                    A(PR[:, n, :], PS[:, 2 + n // 2, (n % 2) * 256:(n % 2) * 256 + 256], ACT.Exp, scale=QSCALE,
                      bias=st[:, n, h:h + 1], accum_out=st[:, n, HEADS + h:HEADS + h + 1]).then_inc(s_p, 1)

            def probs_T(u):
                act.wait_ge(s_pt, u + 1)
                A(PRT[:, 0:4, :], PS[:, 4, :].rearrange("p (k t) -> p k t", k=4), ACT.Copy).then_inc(s_pte, 1)
                A(PRT[:, 4:8, :], PS[:, 5, :].rearrange("p (k t) -> p k t", k=4), ACT.Copy).then_inc(s_pte, 1)

            def items(u):
                return [(u, 0)] if u < 8 else [(8 + 2 * (u - 8), 1), (9 + 2 * (u - 8), 2)]

            for u in range(17):
                for k, (i, g) in enumerate(items(u) if u < 16 else []):
                    if u >= 2:
                        act.wait_ge(s_s, u - 1)
                    qk_copy(i, g, u % 2, k)
                if u >= 2:
                    probs_T(u - 2)
                if u >= 1:
                    softmax(u - 1)
            probs_T(15)
            act.wait_ge(s_st1, 32)
            for d in range(2):
                act.wait_ge(s_dve_w, 2 * d + 2)
                for k in range(2):
                    A(wt[:, d, k, :, :], wt[:, d, k, :, :], ACT.Exp).then_inc(s_wexp, 1)
            for n in range(NT):
                for hf in range(2):
                    act.wait_ge(s_ot, 2 * n + hf + 1)
                    A(OT[:, 4 * hf:4 * hf + 4, n * P:(n + 1) * P],
                      PS[:, 4 + 2 * (n % 2) + hf, :].rearrange("p (h t) -> p h t", h=4), ACT.Copy).then_inc(s_otn, 1)
            norm_round(2)
            moe(1)
            norm_round(3)

        @block.vector
        def _(dve):
            v = nc.vector
            chain = [0]

            def link(ins):
                chain[0] += 1
                ins.then_inc(s_dve, 1)
                dve.wait_ge(s_dve, chain[0])

            def xt_high(q):
                n = q % NT
                if q // NT == 2:
                    dve.wait_ge(s_xta, q + 1)
                    cols = slice(n * P, (n + 1) * P)
                    v.tensor_tensor(XTL[:, :, cols],
                                    PS[:, 4 + 2 * (n % 2):6 + 2 * (n % 2), :].rearrange("p a (k t) -> p (a k) t", k=4),
                                    XTH[:, :, cols].bitcast(F32), ALU.subtract).then_inc(s_xtv, 1)
                    return
                dve.wait_ge(s_xps, q + 1)
                v.tensor_copy(XT[:, 4:8, n * P:(n + 1) * P],
                              PS[:, 5 + 2 * (n % 2), :].rearrange("p (k t) -> p k t", k=4)).then_inc(s_xtv, 1)

            def norm_round(r):
                dve.wait_ge(s_gb, 16 + 32 * (r + 1))
                for n in range(NT):
                    if r % 2 == 0:
                        l = r // 2
                        dve.wait_ge(s_mix[l], n + 1)
                        b = 2 * (n % 2)
                        link(v.scalar_tensor_tensor(X[:, n, :].rearrange("p (a b) -> p a b", a=2),
                                                    X[:, n, :].rearrange("p (a b) -> p a b", a=2), ALPHA,
                                                    PS[:, b:b + 2, :], ALU.mult, ALU.add))
                        if l == 0:
                            link(v.tensor_tensor(X[:, n, :], X[:, n, :], BOUT, ALU.add))
                    else:
                        dve.wait_ge(s_xin[n], 16 * (r // 2 + 2))
                    for h in range(2):
                        last = v.bn_stats(bns[:, h, :], X[:, n, h * 512:(h + 1) * 512])
                    link(last)
                    v.bn_aggr(mv[:, :], bns[:, :, :]).then_inc(s_nvar, 1)
                    dve.wait_ge(s_nstd, NT * r + n + 1)
                    link(v.reciprocal(rstd1[:, :], std1[:, :]))
                    link(v.scalar_tensor_tensor(X[:, n, :], X[:, n, :], mv[:, 0:1], LNG[:, :], ALU.subtract, ALU.mult))
                    v.scalar_tensor_tensor(X[:, n, :], X[:, n, :], rstd1[:, :], LNB[:, :], ALU.mult, ALU.add).then_inc(s_norm, 1)
                    if r < 3 and n >= 1:
                        xt_high(NT * (r + 1) + n - 1)
                if r < 3:
                    xt_high(NT * (r + 1) + NT - 1)

            def route(l):
                dve.wait_ge(s_norm, 2 * NT * l + NT)
                dve.wait_ge(s_rw, 64)
                dve.wait_ge(s_sc, l + 1)
                rb = RB[:, l:l + 1, :].broadcast_to([P, NT, E])
                link(v.tensor_tensor(BI, SC, rb, ALU.add))
                for n in range(NT):
                    last = v.max(m8[:, n, :], BI[:, n, :])
                link(last)
                for n in range(NT):
                    last = v.match_replace(BR[:, n, :], m8[:, n, :], BI[:, n, :], NEG)
                link(last)
                v.tensor_tensor(MK, BI, BR, ALU.not_equal).then_inc(s_mk, 1)
                dve.wait_ge(s_mk, l + 1)
                link(v.tensor_tensor(GS, SC, MK, ALU.mult))
                link(v.tensor_reduce(gsum[:, :], GS, AXX, ALU.add))
                link(v.reciprocal(grec[:, :], gsum[:, :]))
                link(v.tensor_scalar(grec[:, :], grec[:, :], ROUTED_SCALE, None, ALU.mult))
                link(v.tensor_tensor(GT, GS, grec[:, :].unsqueeze(2).broadcast_to([P, NT, E]), ALU.mult))
                dve.wait_ge(s_pos, 2 * l + 2)
                for k in range(3):
                    last = v.tensor_scalar(cnt[:, k:k + 1], PS[0:E, 2, 0:1], float(P * (k + 1)), None, ALU.is_gt)
                link(last)
                link(v.tensor_tensor(cnt[:, 3:4], cnt[:, 0:1], cnt[:, 1:2], ALU.add))
                link(v.tensor_tensor(cnt[:, 3:4], cnt[:, 3:4], cnt[:, 2:3], ALU.add))
                v.tensor_scalar(cntB[:, :], ones[0:E, :], cnt[:, 3:4], None, ALU.mult).then_inc(s_cb, 1)
                dve.wait_ge(s_ob, l + 1)
                link(v.tensor_copy(obs[:, :], PS[:, 2, 128:129 + E]))
                link(v.scalar_tensor_tensor(delta[:, :], obs[:, 0:E], float(P), over_c[:, :], ALU.mult, ALU.add))
                pos = PS[:, 1, 0:256].rearrange("p (n e) -> p n e", n=NT)
                link(v.scalar_tensor_tensor(SLM, pos, float(P), delta[:, :].unsqueeze(1).broadcast_to([P, NT, E]),
                                            ALU.is_ge, ALU.mult))
                link(v.tensor_tensor(SLM, SLM, pos, ALU.add))
                link(v.tensor_tensor(SLM, SLM, base1[:, :].unsqueeze(1).broadcast_to([P, NT, E]), ALU.add))
                link(v.tensor_tensor(SLM, SLM, MK, ALU.mult))
                for n in range(NT):
                    last = v.max(s8[:, n, :], SLM[:, n, :])
                link(last)
                for n in range(NT):
                    last = v.tensor_tensor(EQ[:, n], SLM[:, n:n + 1, :].broadcast_to([P, 8, E]),
                                           s8[:, n, :].unsqueeze(2).broadcast_to([P, 8, E]), ALU.is_equal)
                link(last)
                for n in range(NT):
                    last = v.tensor_tensor(EG[:, n], EQ[:, n], GT[:, n:n + 1, :].broadcast_to([P, 8, E]), ALU.mult)
                link(last)
                link(v.tensor_reduce(g8[:, :, :], EG, AXX, ALU.add))
                s8f = s8[:, :, :].rearrange("p n j -> p (n j)")
                link(v.tensor_scalar(s8i[:, :], s8f, -1.0, None, ALU.add))
                v.tensor_scalar(b8i[:, :], s8i[:, :], 7, None, ALU.logical_shift_right)
                link(v.tensor_scalar(p8i[:, :], s8i[:, :], 127, None, ALU.bitwise_and))
                v.tensor_copy(b8[:, :], b8i[:, :])
                link(v.tensor_copy(p8[:, :], p8i[:, :]))
                for n in range(NT):
                    if n >= 2:
                        dve.wait_ge(s_tb[l], n - 1)
                    s = n % 2
                    b8n, p8n = (a[:, 8 * n:8 * n + 8].unsqueeze(2) for a in (b8, p8))
                    link(v.tensor_tensor(RR[:, s, :, 0:NB], iota_f[:, 0:NB].unsqueeze(1).broadcast_to([P, 8, NB]),
                                         b8n.broadcast_to([P, 8, NB]), ALU.is_equal))
                    v.tensor_tensor(PJ[:, s], iota_f[:, :].unsqueeze(1).broadcast_to([P, 8, P]),
                                    p8n.broadcast_to([P, 8, P]), ALU.is_equal)
                    link(v.tensor_tensor(RR[:, s, :, NB:2 * NB], RR[:, s, :, 0:NB],
                                         g8[:, n, :].unsqueeze(2).broadcast_to([P, 8, NB]), ALU.mult))
                    v.tensor_scalar(RR[:, s, :, 0:NB], RR[:, s, :, 0:NB], pcol[:, 2 + n:3 + n], None,
                                    ALU.mult).then_inc(s_pj[l], 1)
                v.tensor_scalar(tabf[0:32, 0:E], obs[0:32, 1:E + 1], pcol[0:32, 0:1], 0.0,
                                ALU.is_le, ALU.add, accum_out=scratch[0:32, 0:1])
                link(v.tensor_scalar(scratch[0:1, 1:2], obs[0:1, E:E + 1], 1.0, None, ALU.add))
                link(v.tensor_scalar(scratch[0:1, 2:3], scratch[0:1, 1:2], 0.0, None, ALU.add))
                link(v.tensor_scalar(etmp[:, 1:2], scratch[0:32, 0:1], float(E - 1), None, ALU.min))
                link(v.tensor_scalar(etmp[0:1, 0:1], scratch[0:1, 2:3], 0.0, None, ALU.add))
                v.tensor_scalar(extra[0:1, 0:1], etmp[0:1, 0:1], 1, None, ALU.logical_shift_right).then_inc(s_tab, 1)
                dve.wait_ge(s_tb[l], NT)
                link(v.tensor_scalar(tabf[:, :], PS[:, 0, 256:256 + NB], 0.0, pcol[:, 1:2],
                                     ALU.is_equal, ALU.mult))
                link(v.tensor_tensor(tabf[:, :], tabf[:, :], PS[:, 0, 256:256 + NB], ALU.add))
                link(v.tensor_copy(GTAB[:, :], PS[:, 0, 256 + NB:256 + 2 * NB]))
                v.tensor_scalar(IDX[:, :], tabf[:, :], -1.0, None, ALU.add).then_inc(s_tab, 1)

            def moe(l):
                route(l)
                dve.wait_ge(s_tab, 2 * l + 2)
                for m in (2, 3):
                    dve.wait_ge(s_sye[l], 2 * m + 2)
                    dve.wait_ge(s_acc[l][m % 2], 16)
                    v.scalar_tensor_tensor(AXB[:, m % 2, :], X[:, m, :], ALPHA, YS[:, m % 2, :],
                                           ALU.mult, ALU.add).then_inc(s_ax[1], 1)
                n = dve.value_load(extra[0:1, 0:1], min_val=0, max_val=OVER // 2) + E // 2

                dve.wait_ge(s_ax[1], 2 * l + 2)
                dve.wait_ge(s_xr[l], 16 * NT)

                def rows_low(b, s):
                    dve.wait_ge(s_xh[l], b + 1)
                    v.tensor_tensor(XL[:, s, :], PS[:, 0:2, :].rearrange("p a t -> p (a t)"), XH[:, s, :].bitcast(F32),
                                    ALU.subtract).then_inc(s_xl[l], 1)

                def weights_low(b, s):
                    for c in range(2):
                        dve.wait_ge(s_wh[l], b * 2 + 1 + c)
                        v.tensor_tensor(WL[s][:, c, :], W[:, 3 * s + c, :], WH[:, s, c, :].bitcast(F32),
                                        ALU.subtract).then_inc(s_wl[l], 1)

                def hidden(b, s):
                    dve.wait_ge(s_sl[l], b + 1)
                    if not (isinstance(b, int) and b < 2):
                        dve.wait_ge(s_ht[l], b - 1)
                    v.scalar_tensor_tensor(Hm[:, s, :], SLm[:, s, :], GTAB[:, bass.ds(b, 1)], PS[:, 3 + s, F:2 * F],
                                           ALU.mult, ALU.mult).then_inc(s_hd[l], 1)

                def hidden_T(b, s):
                    dve.wait_ge(s_ht[l], b + 1)
                    v.tensor_copy(HTm[:, s, :], PS[:, 2, 0:F]).then_inc(s_he[l], 1)

                def out_high(b, s):
                    dve.wait_ge(s_yd[l], b + 1)
                    if not (isinstance(b, int) and b < 2):
                        dve.wait_ge(s_scat[l], (b - 1) * 16)
                    v.tensor_copy(YB[:, s, 512:D], PS[:, 6, :]).then_inc(s_yv[l], 1)

                def step(b, s, more):
                    hidden_T(b, s)
                    if more:
                        weights_low(b + 2, s)
                    if more or s == 0:
                        hidden(b + 1, 1 - s)
                    if more:
                        rows_low(b + 2, s)
                    out_high(b, s)

                for s in range(2):
                    rows_low(s, s)
                    weights_low(s, s)
                hidden(0, 0)
                step(0, 0, True)
                step(1, 1, True)
                with dve.Fori(1, n - 1) as it:
                    step(it * 2, 0, True)
                    step(it * 2 + 1, 1, True)
                step(n * 2 - 2, 0, False)
                step(n * 2 - 1, 1, False)

            for n in range(NT):
                xt_high(n)
            dve.wait_ge(s_pool, 1)
            link(v.tensor_scalar(imod[:, :], imod[:, :], 3, None, ALU.bitwise_and))
            v.tensor_scalar(mask_far[:, P:256], imod[:, :], 0.0, NEG, ALU.not_equal, ALU.mult).then_inc(s_ang, 1)
            dve.wait_ge(s_posd, 32)
            link(v.tensor_copy(ROT[:, 2, :], POSI.bitcast(I32)))
            link(v.tensor_scalar(ROT[:, 2, :], ROT[:, 2, :], invf[:, :], None, ALU.mult))
            link(v.tensor_scalar(ROT[:, 3, :], ROT[:, 2, :], float(1.0 / (2.0 * np.pi)), None, ALU.mult))
            link(v.tensor_scalar(ROT[:, 3, :], ROT[:, 3, :], MAGIC, None, ALU.add))
            link(v.tensor_scalar(ROT[:, 3, :], ROT[:, 3, :], MAGIC, None, ALU.subtract))
            for c in TWO_PI:
                link(v.scalar_tensor_tensor(ROT[:, 2, :], ROT[:, 3, :], -c, ROT[:, 2, :], ALU.mult, ALU.add))
            v.tensor_scalar(ROT[:, 0, :], ROT[:, 2, :], -PI_LO, PI_LO, ALU.max, ALU.min).then_inc(s_ang, 1)
            link(v.tensor_scalar(ROT[:, 1, :], ROT[:, 2, :], float(np.pi / 2), None, ALU.add))
            link(v.tensor_scalar(ROT[:, 3, :], ROT[:, 1, :], float(np.pi), float(-2.0 * np.pi), ALU.is_gt, ALU.mult))
            link(v.tensor_tensor(ROT[:, 1, :], ROT[:, 1, :], ROT[:, 3, :], ALU.add))
            v.tensor_scalar(ROT[:, 1, :], ROT[:, 1, :], -PI_LO, PI_LO, ALU.max, ALU.min).then_inc(s_ang, 1)
            dve.wait_ge(s_cst, 1)
            dve.wait_ge(s_vev, 2)
            def glu(j):
                dve.wait_ge(s_sg, j + 1)
                v.scalar_tensor_tensor(HP[:, j, HALO:], PS[:, j % 2, :], vecT[:, j:j + 1], SG[:, j % 2, :],
                                       ALU.add, ALU.mult).then_inc(s_h, 1)

            def join(j):
                dve.wait_ge(s_yp, (j + 1) * (POOL_TAPS - 1))
                v.tensor_tensor(Y[:, j, :], Y[:, j, :], Y2[:, 2 * (j % 2), :], ALU.add).then_inc(s_y, 1)

            for j in range(KT):
                glu(j)
                dve.wait_ge(s_h, j + 1)
                if j >= 2:
                    dve.wait_ge(s_y, j - 1)
                for w in range(POOL_TAPS, TAPS):
                    to = Y2[:, 2 * (j % 2) + (w - POOL_TAPS) % 2, :]
                    tap, weight = HP[:, j, w:w + T], dwT[:, j, w:w + 1]
                    if w >= POOL_TAPS + 2:
                        dve.wait_ge(s_dve, chain[0] - 1)
                    chain[0] += 1
                    if w < POOL_TAPS + 2:
                        v.tensor_scalar(to, tap, weight, None, ALU.mult).then_inc(s_dve, 1)
                    else:
                        v.scalar_tensor_tensor(to, tap, weight, to, ALU.mult, ALU.add).then_inc(s_dve, 1)
                    if w == POOL_TAPS + 5 and j >= 1:
                        join(j - 1)
                dve.wait_ge(s_dve, chain[0])
                link(v.tensor_tensor(Y2[:, 2 * (j % 2), :], Y2[:, 2 * (j % 2), :], Y2[:, 2 * (j % 2) + 1, :], ALU.add))
            join(KT - 1)
            dve.wait_ge(s_y, KT)
            dve.wait_ge(s_mu, 1)
            for j in range(KT):
                v.tensor_tensor(Y[:, j, :], Y[:, j, :], PS[:, 4, :], ALU.subtract).then_inc(s_yc, 1)
            dve.wait_ge(s_std, 1)
            link(v.reciprocal(RS, RS))
            for j in range(KT):
                dve.wait_ge(s_sq, KT)
                v.tensor_tensor(Y[:, j, :], Y[:, j, :], RS, ALU.mult).then_inc(s_t, 1)
            norm_round(0)
            moe(0)
            norm_round(1)
            dve.wait_ge(s_trig, 2)
            link(v.tensor_scalar(sinT[:, :], sinT[:, :], sgn[:, :], None, ALU.mult))

            def piece_low(j):
                if j >= len(pieces):
                    return
                dve.wait_ge(s_ph, j + 1)
                v.tensor_tensor(PL[:, j % PIECES, :], RAW[:, j % PIECES, :], PH[:, j % PIECES, :].bitcast(F32),
                                ALU.subtract).then_inc(s_pl, 1)

            for j in range(PIECES - 1):
                piece_low(j)
            for j in range(n_v):
                piece_low(j + PIECES - 1)
                if j % 4 == 3:
                    dve.wait_ge(s_v, j + 1)
                    c = j // 4
                    for n in (1, 3):
                        v.tensor_copy(V[:, c // 2, n, (c % 2) * 512:(c % 2 + 1) * 512], PS[:, 4 * (c % 2) + n, :]).then_inc(s_veh, 1)

            def rotate(i, g, par, item):
                swap = list(range(16, 32)) + list(range(16))
                for w, dst in enumerate((QT, KTT)):
                    piece_low(n_v + 2 * i + w + PIECES - 1)
                    dve.wait_ge(s_qke, 2 * i + w + 1)
                    src = dst[0:32, par, item, :]
                    cs, sn = cosT[:, :], sinT[:, :]
                    r0, r1 = RT[:, 0, :], RT[:, 1, :]
                    if g:
                        cs = cs.rearrange("p (i j) -> p j i", j=NT)
                        sn = sn.rearrange("p (i j) -> p j i", j=NT)
                        r0 = r0.rearrange("p (j i) -> p j i", j=NT)
                        r1 = r1.rearrange("p (j i) -> p j i", j=NT)
                        srcv = src.rearrange("p (j i) -> p j i", j=NT)
                    else:
                        srcv = src
                    if 2 * i + w:
                        dve.wait_ge(s_rot, 2 * i + w)
                    v.stream_shuffle(RT[:, 0, :], src, swap)
                    link(v.tensor_tensor(r1, srcv, cs, ALU.mult))
                    link(v.tensor_tensor(r0, r0, sn, ALU.mult))
                    v.tensor_tensor(src, RT[:, 0, :], RT[:, 1, :], ALU.add).then_inc(s_rot, 1)

            def row_max(u):
                st = statN[:, 0] if u < 8 else statP[:, 1]
                h = u % 8
                S = PS[:, 2:4, :].rearrange("p a (n c) -> p (a n) c", n=2)
                dve.wait_ge(s_s, u + 1)
                if u < 8:
                    v.tensor_tensor(S[:, 0, :], S[:, 0, :], mask_first[:, :], ALU.add)
                    link(v.tensor_tensor(S[:, 1:4, :], S[:, 1:4, :], mask_near[:, :].unsqueeze(1).broadcast_to([P, 3, 256]),
                                         ALU.add))
                else:
                    link(v.tensor_tensor(S, S, mask_far[:, :].unsqueeze(1).broadcast_to([P, 4, 256]), ALU.add))
                link(v.tensor_reduce(mx[:, :], S, AXX, ALU.max))
                v.tensor_scalar(st[:, :, h], mx[:, :], -QSCALE, None, ALU.mult).then_inc(s_m, 1)

            def pv_copy(u):
                dst = O0 if u < 8 else O12
                h = u % 8
                dve.wait_ge(s_o, u + 1)
                v.tensor_copy(dst[:, :, h * P:(h + 1) * P], PS[:, 6, :].rearrange("p (n d) -> p n d", n=NT)).then_inc(s_oe, 1)

            def items(u):
                return [(u, 0)] if u < 8 else [(8 + 2 * (u - 8), 1), (9 + 2 * (u - 8), 2)]

            for u in range(17):
                for k, (i, g) in enumerate(items(u) if u < 16 else []):
                    rotate(i, g, u % 2, k)
                if u >= 1:
                    row_max(u - 1)
                if u >= 2:
                    pv_copy(u - 2)
            pv_copy(15)
            dve.wait_ge(s_st1, 32)
            dve.wait_ge(s_p, 64)
            for d, st in enumerate((statN, statP)):
                link(v.tensor_tensor(wt[:, d, 2], st[:, 0, :, 0:HEADS], st[:, 1, :, 0:HEADS], ALU.min))
                for k in range(2):
                    v.tensor_tensor(wt[:, d, k], wt[:, d, 2], st[:, k, :, 0:HEADS], ALU.subtract).then_inc(s_dve_w, 1)
            for d, st in enumerate((statN, statP)):
                dve.wait_ge(s_wexp, 2 * d + 2)
                for k in range(2):
                    last = v.tensor_tensor(wt[:, d, 2 + k], wt[:, d, k], st[:, k, :, HEADS:2 * HEADS], ALU.mult)
                link(last)
                link(v.tensor_tensor(wt[:, d, 2], wt[:, d, 2], wt[:, d, 3], ALU.add))
                link(v.reciprocal(wt[:, d, 2], wt[:, d, 2]))
                link(v.tensor_tensor(wt[:, d, 3], wt[:, d, d], wt[:, d, 2], ALU.mult))
            for d, o in enumerate((O0, O12)):
                for n in range(NT):
                    on = o[:, n, :].rearrange("p (h c) -> p h c", h=HEADS)
                    v.tensor_tensor(on, on, wt[:, d, 3, n, :].unsqueeze(2).broadcast_to([P, HEADS, P]),
                                    ALU.mult).then_inc(s_wts, 1)
            dve.wait_ge(s_otn, 2 * NT)
            for n in range(NT):
                for hf in range(2):
                    c = NT + n
                    dve.wait_ge(s_ot, 2 * c + hf + 1)
                    src = PS[:, 4 + 2 * (c % 2) + hf, :].rearrange("p (h t) -> p h t", h=4)
                    dst = OT[:, 4 * hf:4 * hf + 4, :].rearrange("p h (i j) -> p h j i", j=NT)[:, :, n, :]
                    v.tensor_tensor(dst, dst, src, ALU.add).then_inc(s_ote, 1)
            norm_round(2)
            moe(1)
            norm_round(3)

        @block.tensor
        def _(pe):
            mm = nc.tensor.matmul

            def x_T(q):
                r, n = q // NT, q % NT
                if r == 0:
                    pe.wait_ge(s_xin[n], 16)
                else:
                    pe.wait_ge(s_norm, NT * (r - 1) + n + 1)
                if q >= 2:
                    pe.wait_ge(s_xta, q - 1)
                    pe.wait_ge(s_xtv, q - 1)
                for k in range(KT):
                    last = nc.tensor.transpose(PS[:, 4 + 2 * (n % 2) + k // 4, (k % 4) * P:(k % 4 + 1) * P],
                                               X[:, n, k * P:(k + 1) * P], ident[:, :])
                last.then_inc(s_xps, 1)

            def out_proj(l, lhs, key):
                for c in range(4):
                    landed(pe, (key, c))
                for n in range(NT):
                    if n >= 2:
                        pe.wait_ge(s_norm, 2 * NT * l + n - 1)
                    for h in range(2):
                        for k in range(KT):
                            last = mm(PS[:, 2 * (n % 2) + h, :].rearrange("p (a b) -> p a b", a=2),
                                      lhs[:, k, n * P:(n + 1) * P], pair((key, 2 * h), k), start=(k == 0), stop=(k == KT - 1))
                    last.then_inc(s_mix[l], 1)
                    if n >= 2:
                        x_T(NT * (2 * l + 1) + n - 2)

            def x_T_and_router(l):
                pe.wait_ge(s_rw, 64)

                def router(n):
                    pe.wait_ge(s_xta, NT * (2 * l + 1) + n + 1)
                    pe.wait_ge(s_xtv, NT * (2 * l + 1) + n + 1)
                    for k in range(KT):
                        last = mm(PS[:, 0, n * E:(n + 1) * E], XT[:, k, n * P:(n + 1) * P], RW[:, l, k, :],
                                  start=(k == 0), stop=(k == KT - 1))
                    if n == NT - 1:
                        last.then_inc(s_rt, 1)

                x_T(NT * (2 * l + 1) + 2)
                router(0)
                router(1)
                x_T(NT * (2 * l + 1) + 3)
                router(2)
                router(3)

            def moe(l):
                def sh_gate_up(n):
                    if n == 0:
                        landed(pe, ("sg", l))
                        landed(pe, ("su", l))
                    if n >= 2:
                        pe.wait_ge(s_ssl[l], 2 * (n - 1))
                    for k in range(KT):
                        last = mm(PS[:, 4 + n % 2, :].rearrange("p (a b) -> p a b", a=2), XT[:, k, n * P:(n + 1) * P],
                                  pair(("sg", l), k), start=(k == 0), stop=(k == KT - 1))
                    last.then_inc(s_sgu[l], 1)

                def sh_down(n):
                    if n == 0:
                        landed(pe, ("sd", l))
                    pe.wait_ge(s_sh[l], n + 1)
                    if n >= 1:
                        pe.wait_ge(s_she[l], n)
                    for k in range(2):
                        last = nc.tensor.transpose(PS[:, 6, k * P:(k + 1) * P], HSs[:, n % 2, k * P:(k + 1) * P], ident[:, :])
                    last.then_inc(s_sht[l], 1)
                    pe.wait_ge(s_she[l], n + 1)
                    wd = chunk(("sd", l), 2)
                    for h in range(2):
                        if n >= 1:
                            pe.wait_ge(s_sye[l], 2 * (n - 1) + h + 1)
                        for k in range(2):
                            last = mm(PS[:, 7 if h == 0 else 3, :], HTs[:, n % 2, k * P:(k + 1) * P],
                                      wd[:, k, h * 512:(h + 1) * 512], start=(k == 0), stop=(k == 1))
                        last.then_inc(s_sy[l], 1)

                sh_gate_up(0)
                pe.wait_ge(s_mk, l + 1)
                for n in range(NT):
                    for m in range(n):
                        mm(PS[:, 1, n * E:(n + 1) * E], ones[:, :], MK[:, m, :], start=(m == 0), stop=False)
                    last = mm(PS[:, 1, n * E:(n + 1) * E], before[:, :], MK[:, n, :], start=(n == 0), stop=True)
                last.then_inc(s_pos, 1)
                for n in range(NT):
                    last = mm(PS[0:E, 2, 0:2], MK[:, n, :], ones[:, 0:2], start=(n == 0), stop=(n == NT - 1))
                last.then_inc(s_pos, 1)
                sh_gate_up(1)
                pe.wait_ge(s_cb, l + 1)
                mm(PS[:, 2, 128:128 + E], cntB[:, :], before[0:E, 0:E], start=True, stop=True)
                mm(PS[:, 2, 128 + E:130 + E], cntB[:, :], ones[0:E, 0:2], start=True, stop=True).then_inc(s_ob, 1)
                sh_down(0)
                sh_gate_up(2)
                sh_down(1)
                sh_gate_up(3)
                for n in range(NT):
                    pe.wait_ge(s_pj[l], n + 1)
                    for j in range(8):
                        last = mm(PS[:, 0, 256:256 + 2 * NB], PJ[:, n % 2, j, :], RR[:, n % 2, j, :],
                                  start=(n == 0 and j == 0), stop=(n == NT - 1 and j == 7))
                    last.then_inc(s_tb[l], 1)
                sh_down(2)
                sh_down(3)
                pe.wait_ge(s_tab, 2 * l + 2)
                pe.wait_ge(s_sye[l], 2 * NT)
                n = pe.value_load(extra[0:1, 0:1], min_val=0, max_val=OVER // 2) + E // 2

                def rows_T(b, s, it):
                    pe.wait_ge(s_ga[l][s], it * 16 + 16)
                    if not (isinstance(b, int) and b == 0):
                        pe.wait_ge(s_xl[l], b)
                    for k in range(KT):
                        last = nc.tensor.transpose(PS[:, k // 4, (k % 4) * P:(k % 4 + 1) * P],
                                                   XG[:, s, :].rearrange("p (c k) -> p k c", k=KT)[:, k, :], ident[:, :])
                    last.then_inc(s_tx[l], 1)

                def gate_up(b, s):
                    pe.wait_ge(s_xl[l], b + 1)
                    pe.wait_ge(s_wl[l], b * 2 + 2)
                    if not (isinstance(b, int) and b < 2):
                        pe.wait_ge(s_hd[l], b - 1)
                    for k in range(KT):
                        xh, xl = XH[:, s, k * P:(k + 1) * P], XL[:, s, k * P:(k + 1) * P]
                        wh, wl = WH[:, s, :, k * F:(k + 1) * F], WL[s][:, :, k * F:(k + 1) * F]
                        for i, (a, w) in enumerate(((xh, wh), (xh, wl), (xl, wh))):
                            last = mm(PS[:, 3 + s, :].rearrange("p (a b) -> p a b", a=2), a, w,
                                      start=(k == 0 and i == 0), stop=(k == KT - 1 and i == 2))
                    last.then_inc(s_gu[l], 1)

                def hidden_T(b, s):
                    pe.wait_ge(s_hd[l], b + 1)
                    if not (isinstance(b, int) and b == 0):
                        pe.wait_ge(s_he[l], b)
                    for k in range(2):
                        last = nc.tensor.transpose(PS[:, 2, k * P:(k + 1) * P], Hm[:, s, k * P:(k + 1) * P], ident[:, :])
                    last.then_inc(s_ht[l], 1)

                def down_proj(b, s, it):
                    pe.wait_ge(s_he[l], b + 1)
                    pe.wait_ge(s_mw[l][3 * s + 2], it * 16 + 16)
                    if not (isinstance(b, int) and b == 0):
                        pe.wait_ge(s_ya[l], b)
                        pe.wait_ge(s_yv[l], b)
                    wd = W[:, 3 * s + 2, :].rearrange("p (k n) -> p k n", k=2)
                    for h in range(2):
                        for k in range(2):
                            last = mm(PS[:, 5 + h, :], HTm[:, s, k * P:(k + 1) * P], wd[:, k, h * 512:(h + 1) * 512],
                                      start=(k == 0), stop=(k == 1))
                    last.then_inc(s_yd[l], 1)

                def step(b, s, it, more):
                    hidden_T(b, s)
                    if more or s == 0:
                        gate_up(b + 1, 1 - s)
                    if more:
                        rows_T(b + 2, s, it + 1)
                    down_proj(b, s, it)

                rows_T(0, 0, 0)
                rows_T(1, 1, 0)
                gate_up(0, 0)
                step(0, 0, 0, True)
                step(1, 1, 0, True)
                with pe.Fori(1, n - 1) as it:
                    step(it * 2, 0, it, True)
                    step(it * 2 + 1, 1, it, True)
                step(n * 2 - 2, 0, n - 1, False)
                step(n * 2 - 1, 1, n - 1, False)

            pe.wait_ge(s_cst, 1)
            pe.wait_ge(s_vec, 16 * 5)
            nc.tensor.transpose(PS[:, 0, 0:40], vec_rows[:, :], ident[0:40, 0:40])
            for k in range(KT):
                last = nc.tensor.transpose(PS[:, 1, k * TAPS:(k + 1) * TAPS], DWR[:, k * P:(k + 1) * P], ident[0:TAPS, 0:TAPS])
            last.then_inc(s_vps, 1)
            for n in range(NT):
                x_T(n)
            pe.wait_ge(s_vev, 2)
            pe.wait_ge(s_xta, NT)
            pe.wait_ge(s_xtv, NT)
            for j in range(KT):
                m, c = j // 2, (j % 2) * P
                if j >= 2:
                    pe.wait_ge(s_h, j - 1)
                for key, bank in (("a", j % 2), ("g", 2 + j % 2)):
                    if j % 2 == 0:
                        landed(pe, (key, m))
                    for k in range(KT):
                        last = mm(PS[:, bank, :], chunk((key, m))[:, k, c:c + P], XT[:, k, :], start=(k == 0), stop=(k == KT - 1))
                last.then_inc(s_ag, 1)
            for j in range(KT):
                pe.wait_ge(s_y, j + 1)
                last = mm(PS[:, 4, :], inv_d[:, :], Y[:, j, :], start=(j == 0), stop=(j == KT - 1))
            last.then_inc(s_mu, 1)
            for j in range(KT):
                pe.wait_ge(s_sq, j + 1)
                mm(PS[:, 5, :], inv_d[:, :], SQ[:, j % 2, :], start=(j == 0), stop=(j == KT - 1)).then_inc(s_vm, 1)
            pe.wait_ge(s_z, KT)
            out_proj(0, Y, "co")
            x_T_and_router(0)
            moe(0)
            for n in range(NT):
                x_T(2 * NT + n)
            pe.wait_ge(s_xta, 3 * NT)
            pe.wait_ge(s_xtv, 3 * NT)
            for j in range(n_v):
                c, q = j // 4, j % 4
                if q == 0 and c >= 2:
                    pe.wait_ge(s_ve, 2 * (c - 1))
                    pe.wait_ge(s_veh, 2 * (c - 1))
                pe.wait_ge(s_pl, j + 1)
                for k in (2 * q, 2 * q + 1):
                    wh, wl = (w[:, j % PIECES, (k % 2) * 512:(k % 2 + 1) * 512] for w in (PH, PL))
                    for n in range(NT):
                        xh, xl = (a[:, k, n * P:(n + 1) * P] if c < 2 else a[:, k, :].rearrange("p (i j) -> p j i", j=NT)[:, n, :]
                                  for a in (XTH, XTL))
                        for i, (a, w) in enumerate(((xh, wh), (xh, wl), (xl, wh))):
                            last = mm(PS[:, 4 * (c % 2) + n, :], a, w, start=(k == 0 and i == 0), stop=(k == KT - 1 and i == 2))
                last.then_inc(s_v, 1)

            def items(u):
                return [(u, 0)] if u < 8 else [(8 + 2 * (u - 8), 1), (9 + 2 * (u - 8), 2)]

            def project(u):
                for i, g in items(u):
                    for w in range(2):
                        j = n_v + 2 * i + w
                        pe.wait_ge(s_pl, j + 1)
                        if i >= 1:
                            pe.wait_ge(s_qke, 2 * (i - 1) + w + 1)
                        for k in range(KT):
                            wh, wl = (a[:, j % PIECES, k * P:(k + 1) * P] for a in (PH, PL))
                            for t, (a, b) in enumerate(((wh, XTH), (wh, XTL), (wl, XTH))):
                                last = mm(PS[:, w, :], a, b[:, k, :], start=(k == 0 and t == 0), stop=(k == KT - 1 and t == 2))
                        last.then_inc(s_qk, 1)

            def scores(u):
                par = u % 2
                i = items(u)[-1][0]
                pe.wait_ge(s_rot, 2 * (i + 1))
                if u >= 1:
                    pe.wait_ge(s_p, 4 * u)
                for n in range(NT):
                    for half in range(2):
                        item = half if u >= 8 else 0
                        kn = n if (u >= 8 or half == 1 or n == 0) else n - 1
                        last = mm(PS[:, 2 + n // 2, (n % 2) * 256 + half * P:(n % 2) * 256 + (half + 1) * P],
                                  QT[:, par, item, n * P:(n + 1) * P], KTT[:, par, item, kn * P:(kn + 1) * P],
                                  start=True, stop=True)
                last.then_inc(s_s, 1)

            def probs_T(u):
                pe.wait_ge(s_p, 4 * u + 4)
                if u >= 1:
                    pe.wait_ge(s_pte, 2 * u)
                for n in range(NT):
                    for half in range(2):
                        c = 2 * n + half
                        last = nc.tensor.transpose(PS[:, 4 + c // 4, (c % 4) * P:(c % 4 + 1) * P],
                                                   PR[:, n, half * P:(half + 1) * P], ident[:, :])
                last.then_inc(s_pt, 1)

            def pv(u):
                h = u % 8
                pe.wait_ge(s_pte, 2 * u + 2)
                if u >= 1:
                    pe.wait_ge(s_oe, u)
                for n in range(NT):
                    for half in range(2):
                        g = 0 if u < 8 else 1 + half
                        kn = n if (u >= 8 or half == 1 or n == 0) else n - 1
                        last = mm(PS[:, 6, n * P:(n + 1) * P], PRT[:, 2 * n + half, :], V[:, g, kn, h * P:(h + 1) * P],
                                  start=(half == 0), stop=(half == 1))
                last.then_inc(s_o, 1)

            pe.wait_ge(s_ve, 10)
            pe.wait_ge(s_veh, 10)
            project(0)
            pe.wait_ge(s_ve, 12)
            pe.wait_ge(s_veh, 12)
            for u in range(16):
                if u < 15:
                    project(u + 1)
                if u >= 1:
                    probs_T(u - 1)
                scores(u)
                if u >= 1:
                    pv(u - 1)
            probs_T(15)
            pv(15)
            for c in range(2 * NT):
                o, n = (O0, O12)[c // NT], c % NT
                pe.wait_ge(s_wts, c + 1)
                if 2 <= c < NT + 2:
                    pe.wait_ge(s_otn, 2 * (c - 1))
                elif c >= 2:
                    pe.wait_ge(s_ote, 2 * (c - 1 - NT))
                for hf in range(2):
                    for h in range(4):
                        last = nc.tensor.transpose(PS[:, 4 + 2 * (c % 2) + hf, h * P:(h + 1) * P],
                                                   o[:, n, (4 * hf + h) * P:(4 * hf + h + 1) * P], ident[:, :])
                    last.then_inc(s_ot, 1)
            pe.wait_ge(s_ote, 2 * NT)
            out_proj(1, OT, "ao")
            x_T_and_router(1)
            moe(1)


_INS = ["x", "positions", "ln1_g", "ln1_b", "ln2_g", "ln2_b", "conv_w_in", "conv_b_in", "conv_w_dw", "conv_b_dw",
        "conv_ln_g", "conv_ln_b", "conv_w_out", "conv_b_out", "w_kv", "attn_w_q", "attn_w_o", "router_w",
        "router_bias", "exp_w_gate", "exp_w_up", "exp_w_down", "sh_w_gate", "sh_w_up", "sh_w_down"]


def kernel(**inputs):
    import concourse.bacc as bacc
    from concourse.bass_utils import run_bass_kernel_spmd

    nc = bacc.Bacc("TRN2", target_bir_lowering=False, num_devices=1)
    arrays, args = {}, []
    for name in _INS:
        a = np.ascontiguousarray(inputs[name])
        arrays[f"in_{name}"] = a
        args.append(nc.dram_tensor(f"in_{name}", a.shape, mybir.dt.from_np(a.dtype), kind="ExternalInput").ap())
    freq = np.float32(500000.0) ** (-np.arange(16, dtype=np.float32) * np.float32(2.0) / np.float32(32.0))
    arrays["inv_freq"] = np.concatenate([freq, freq]).astype(np.float32).reshape(32, 1)
    args.append(nc.dram_tensor("inv_freq", (32, 1), F32, kind="ExternalInput").ap())
    args.append(nc.dram_tensor("out", (1, T, D), F32, kind="ExternalOutput").ap())
    build(nc, *args)
    r = run_bass_kernel_spmd(nc, [arrays], core_ids=[0])
    return r.results[0]["out"]
```
